# Optimizing a Trainium2 kernel written in Bass

```python
import jax, jax.numpy as jnp
from jax import lax
import numpy as np

D_MODEL = 1024
BATCH = 1
SEQ = 1024
DEPTH = 1
DEC_BATCH = 8
DEC_SEQ = 8
PAST_LEN = 8192
PAGE_SIZE = 128

A_HEADS = 4
A_HEAD_DIM = (3 * D_MODEL // 8) // A_HEADS
D_A = A_HEADS * A_HEAD_DIM
CHUNK = 128
D_B = 3 * D_MODEL // 8
CONV_W = 3
D_C = D_MODEL - D_A - D_B
POOL_WINDOWS = (2, 4, 8, 16)
N_POOL = len(POOL_WINDOWS)
C_GROUP = D_C // N_POOL
POOL_BUF = max(POOL_WINDOWS) - 1
OFF_AU = 0
OFF_AV = OFF_AU + D_A
OFF_BB = OFF_AV + D_A
OFF_BC = OFF_BB + D_B
OFF_BX = OFF_BC + D_B
OFF_CZ = OFF_BX + D_B
D_IN = OFF_CZ + D_C
MEM_LEN = 256
X_HEADS = 4
X_HEAD_DIM = D_MODEL // X_HEADS
N_GROUPS = 4
EXP_PER_GROUP = 8
TOP_K = 2
D_EXPERT = D_MODEL // 4
EPS = 1e-6

kernel_name = "hymba_style_chunkmlp_conv_pool_hmoe_step"

def rmsnorm(x, g):
    xf = x.astype(jnp.float32)
    y = xf * lax.rsqrt(jnp.mean(xf * xf, axis=-1, keepdims=True) + EPS)
    return (y * g.astype(jnp.float32)).astype(x.dtype)

def layernorm(x, g, b):
    xf = x.astype(jnp.float32)
    mu = jnp.mean(xf, axis=-1, keepdims=True)
    xc = xf - mu
    var = jnp.mean(xc * xc, axis=-1, keepdims=True)
    return (xc * lax.rsqrt(var + EPS) * g.astype(jnp.float32) + b.astype(jnp.float32)).astype(x.dtype)

def chunk_gate(u, v, w_s, b_s):
    n, t, _ = v.shape
    L = min(t, CHUNK)
    nc = t // L
    mask = jnp.tril(jnp.ones((L, L), dtype=bool))
    w = jnp.where(mask[None], w_s[:, :L, :L], jnp.zeros((), w_s.dtype))
    vh = v.reshape(n, nc, L, A_HEADS, A_HEAD_DIM)
    mixed = jnp.einsum('hij,ncjhd->ncihd', w, vh) + jnp.transpose(b_s[:, :L])[None, None, :, :, None]
    return u * mixed.reshape(n, t, D_A)

def short_conv(z, buf, w_conv):
    t = z.shape[1]
    zp = jnp.concatenate([buf, z], axis=1)
    y = w_conv[0] * zp[:, 0:t]
    for k in range(1, CONV_W):
        y = y + w_conv[k] * zp[:, k:k + t]
    return y, zp[:, -(CONV_W - 1):]

def pool_mix(z, buf, start, w_pool, s_pool):
    n, t, _ = z.shape
    zp = jnp.concatenate([buf, z], axis=1)
    cs = jnp.cumsum(zp.astype(jnp.float32), axis=1)
    cs = jnp.concatenate([jnp.zeros_like(cs[:, :1]), cs], axis=1)
    pos = start + jnp.arange(t)
    end = cs[:, POOL_BUF + 1:]
    means = []
    for g, w in enumerate(POOL_WINDOWS):
        lo, hi = g * C_GROUP, (g + 1) * C_GROUP
        s = end[:, :, lo:hi] - cs[:, POOL_BUF + 1 - w:POOL_BUF + 1 - w + t, lo:hi]
        cnt = jnp.minimum(pos + 1, w).astype(jnp.float32)
        means.append(s / cnt[None, :, None])
    mean = jnp.concatenate(means, axis=-1).astype(z.dtype)
    d = (mean - z).reshape(n, t, N_POOL, C_GROUP)
    y = jnp.einsum('ntgc,gce->ntge', d, w_pool).reshape(n, t, D_C) * s_pool
    return y, zp[:, -POOL_BUF:]

def mem_kv(mem, w_xk, w_xv):
    k = jnp.einsum('nmd,dhe->nmhe', mem, w_xk.reshape(D_MODEL, X_HEADS, X_HEAD_DIM))
    v = jnp.einsum('nmd,dhe->nmhe', mem, w_xv.reshape(D_MODEL, X_HEADS, X_HEAD_DIM))
    return k, v

def cross_attn(h, k, v, w_xq, w_xo):
    n, t, _ = h.shape
    q = jnp.einsum('ntd,dhe->nthe', h, w_xq.reshape(D_MODEL, X_HEADS, X_HEAD_DIM))
    s = jnp.einsum('nthe,nmhe->nhtm', q, k).astype(jnp.float32) * (X_HEAD_DIM ** -0.5)
    p = jax.nn.softmax(s, axis=-1).astype(v.dtype)
    o = jnp.einsum('nhtm,nmhe->nthe', p, v).reshape(n, t, D_MODEL)
    return o @ w_xo

def hier_moe(x, w_rg, b_rg, w_re, b_re, w_e1, w_e3, w_e2):
    n, t, d = x.shape
    xf = x.reshape(n * t, d)
    g_logits = (xf @ w_rg + b_rg).astype(jnp.float32)
    g_prob = jax.nn.softmax(g_logits, axis=-1)
    g_idx = jnp.argmax(g_logits, axis=-1)
    g_gate = jnp.take_along_axis(g_prob, g_idx[:, None], axis=-1)
    e_logits = (jnp.einsum('nd,dge->nge', xf, w_re) + b_re).astype(jnp.float32)
    e_sel = jnp.take_along_axis(e_logits, g_idx[:, None, None], axis=1)[:, 0]
    top_v, top_i = lax.top_k(e_sel, TOP_K)
    top_w = jax.nn.softmax(top_v, axis=-1) * g_gate
    e_gate = jnp.sum(top_w[..., None] * jax.nn.one_hot(top_i, EXP_PER_GROUP, dtype=jnp.float32), axis=1)
    gates = (jax.nn.one_hot(g_idx, N_GROUPS, dtype=jnp.float32)[:, :, None] * e_gate[:, None, :]).astype(x.dtype)
    y = jnp.zeros_like(xf)
    for g in range(N_GROUPS):
        a = jnp.einsum('nd,edf->nef', xf, w_e1[g])
        b = jnp.einsum('nd,edf->nef', xf, w_e3[g])
        hid = jax.nn.silu(a) * b * gates[:, g, :, None]
        y = y + jnp.einsum('nef,efd->nd', hid, w_e2[g])
    return y.reshape(n, t, d)

def trunk_layer(x, conv_buf, pool_buf, mem_k, mem_v, start,
                g_mix, w_in, ln_a_g, ln_a_b, w_s, b_s, w_conv, w_pool, s_pool, w_out,
                g_x, w_xq, w_xo, g_ffn, w_rg, b_rg, w_re, b_re, w_e1, w_e3, w_e2):
    n, t, _ = x.shape
    p = rmsnorm(x, g_mix) @ w_in
    a_u = jax.nn.gelu(p[..., OFF_AU:OFF_AV])
    a_v = layernorm(jax.nn.gelu(p[..., OFF_AV:OFF_BB]), ln_a_g, ln_a_b)
    y_a = chunk_gate(a_u, a_v, w_s, b_s)
    z_b = p[..., OFF_BC:OFF_BX] * p[..., OFF_BX:OFF_CZ]
    conv, new_conv = short_conv(z_b, conv_buf, w_conv)
    y_b = p[..., OFF_BB:OFF_BC] * conv
    y_c, new_pool = pool_mix(p[..., OFF_CZ:D_IN], pool_buf, start, w_pool, s_pool)
    x = x + jnp.concatenate([y_a, y_b, y_c], axis=-1) @ w_out
    x = x + cross_attn(rmsnorm(x, g_x), mem_k, mem_v, w_xq, w_xo)
    x = x + hier_moe(rmsnorm(x, g_ffn), w_rg, b_rg, w_re, b_re, w_e1, w_e3, w_e2)
    return x, new_conv, new_pool, a_v

def setup_inputs(seed: int = 0) -> dict:
    key = jax.random.key(seed)
    ks = jax.random.split(key, 40)
    f32 = jnp.float32

    def nrm(k, shape, scale):
        return jax.random.normal(k, shape, f32) * scale

    return {
        'x_prompt': nrm(ks[0], (BATCH, SEQ, D_MODEL), 1.0),
        'x_sample': nrm(ks[1], (DEC_BATCH, DEC_SEQ, D_MODEL), 1.0),
        'mem_prompt': nrm(ks[2], (BATCH, MEM_LEN, D_MODEL), 1.0),
        'state_conv': nrm(ks[3], (DEPTH, DEC_BATCH, CONV_W - 1, D_B), 1.0),
        'state_pool': nrm(ks[4], (DEPTH, DEC_BATCH, POOL_BUF, D_C), 1.0),
        'cache_mem_k': nrm(ks[5], (DEPTH, DEC_BATCH, MEM_LEN, X_HEADS, X_HEAD_DIM), 1.0),
        'cache_mem_v': nrm(ks[6], (DEPTH, DEC_BATCH, MEM_LEN, X_HEADS, X_HEAD_DIM), 1.0),
        'g_mix': 1.0 + nrm(ks[7], (DEPTH, D_MODEL), 0.1),
        'w_in': nrm(ks[8], (DEPTH, D_MODEL, D_IN), D_MODEL ** -0.5),
        'ln_a_g': 1.0 + nrm(ks[9], (DEPTH, D_A), 0.1),
        'ln_a_b': nrm(ks[10], (DEPTH, D_A), 0.02),
        'w_s': nrm(ks[11], (DEPTH, A_HEADS, CHUNK, CHUNK), CHUNK ** -0.5),
        'b_s': 1.0 + nrm(ks[12], (DEPTH, A_HEADS, CHUNK), 0.1),
        'w_conv': nrm(ks[13], (DEPTH, CONV_W, D_B), CONV_W ** -0.5),
        'w_pool': nrm(ks[14], (DEPTH, N_POOL, C_GROUP, C_GROUP), C_GROUP ** -0.5),
        's_pool': 1.0 + nrm(ks[15], (DEPTH, D_C), 0.1),
        'w_out': nrm(ks[16], (DEPTH, D_MODEL, D_MODEL), D_MODEL ** -0.5),
        'w_xk': nrm(ks[17], (DEPTH, D_MODEL, D_MODEL), D_MODEL ** -0.5),
        'w_xv': nrm(ks[18], (DEPTH, D_MODEL, D_MODEL), D_MODEL ** -0.5),
        'g_x': 1.0 + nrm(ks[19], (DEPTH, D_MODEL), 0.1),
        'w_xq': nrm(ks[20], (DEPTH, D_MODEL, D_MODEL), D_MODEL ** -0.5),
        'w_xo': nrm(ks[21], (DEPTH, D_MODEL, D_MODEL), D_MODEL ** -0.5),
        'g_ffn': 1.0 + nrm(ks[22], (DEPTH, D_MODEL), 0.1),
        'w_rg': nrm(ks[23], (DEPTH, D_MODEL, N_GROUPS), D_MODEL ** -0.5),
        'b_rg': nrm(ks[24], (DEPTH, N_GROUPS), 0.01),
        'w_re': nrm(ks[25], (DEPTH, D_MODEL, N_GROUPS, EXP_PER_GROUP), D_MODEL ** -0.5),
        'b_re': nrm(ks[26], (DEPTH, N_GROUPS, EXP_PER_GROUP), 0.01),
        'w_e1': nrm(ks[27], (DEPTH, N_GROUPS, EXP_PER_GROUP, D_MODEL, D_EXPERT), D_MODEL ** -0.5),
        'w_e3': nrm(ks[28], (DEPTH, N_GROUPS, EXP_PER_GROUP, D_MODEL, D_EXPERT), D_MODEL ** -0.5),
        'w_e2': nrm(ks[29], (DEPTH, N_GROUPS, EXP_PER_GROUP, D_EXPERT, D_MODEL), D_EXPERT ** -0.5),
        'g_final': 1.0 + nrm(ks[30], (D_MODEL,), 0.1),
    }

def reference(x_prompt, x_sample, mem_prompt, state_conv, state_pool, cache_mem_k, cache_mem_v,
              g_mix, w_in, ln_a_g, ln_a_b, w_s, b_s, w_conv, w_pool, s_pool, w_out,
              w_xk, w_xv, g_x, w_xq, w_xo, g_ffn, w_rg, b_rg, w_re, b_re, w_e1, w_e3, w_e2,
              g_final):
    xp, xs = x_prompt, x_sample
    conv_p, conv_s, pool_p, pool_s, v_s, mk_p, mv_p = [], [], [], [], [], [], []
    for l in range(DEPTH):
        w = (g_mix[l], w_in[l], ln_a_g[l], ln_a_b[l], w_s[l], b_s[l], w_conv[l], w_pool[l],
             s_pool[l], w_out[l], g_x[l], w_xq[l], w_xo[l], g_ffn[l], w_rg[l], b_rg[l],
             w_re[l], b_re[l], w_e1[l], w_e3[l], w_e2[l])
        mk, mv = mem_kv(mem_prompt, w_xk[l], w_xv[l])
        zc = jnp.zeros((BATCH, CONV_W - 1, D_B), xp.dtype)
        zpool = jnp.zeros((BATCH, POOL_BUF, D_C), xp.dtype)
        xp, c_p, p_p, _ = trunk_layer(xp, zc, zpool, mk, mv, 0, *w)
        xs, c_s, p_s, av_s = trunk_layer(xs, state_conv[l], state_pool[l], cache_mem_k[l],
                                         cache_mem_v[l], PAST_LEN, *w)
        conv_p.append(c_p); conv_s.append(c_s); pool_p.append(p_p); pool_s.append(p_s)
        v_s.append(av_s); mk_p.append(mk); mv_p.append(mv)
    y_prompt = rmsnorm(xp, g_final)
    y_sample = rmsnorm(xs, g_final)
    new_conv_prompt = jnp.stack(conv_p)
    new_conv_sample = jnp.stack(conv_s)
    new_pool_prompt = jnp.stack(pool_p)
    new_pool_sample = jnp.stack(pool_s)
    new_chunk_v_sample = jnp.stack(v_s)
    new_mem_k_prompt = jnp.stack(mk_p)
    new_mem_v_prompt = jnp.stack(mv_p)
    return (y_prompt, y_sample, new_conv_prompt, new_conv_sample, new_pool_prompt,
            new_pool_sample, new_chunk_v_sample, new_mem_k_prompt, new_mem_v_prompt)


_drawn_inputs = setup_inputs


def setup_inputs(seed=0):
    import zlib

    import numpy as np

    out = dict(_drawn_inputs(seed))
    spreads = {}
    factors = {'ln_a_b': 2.917, 'g_x': 3.781, 'b_rg': 13.549, 'b_re': 5.396}
    for name, (base, spread) in spreads.items():
        noise = np.random.default_rng([zlib.crc32(name.encode()), seed]).standard_normal(out[name].shape)
        drawn = base * np.exp(spread * noise) if base else spread * noise
        out[name] = __import__('jax').numpy.asarray(drawn.astype(out[name].dtype))
    for name, factor in factors.items():
        out[name] = (out[name] * factor).astype(out[name].dtype)
    return out
```

```python
from contextlib import ExitStack

import numpy as np

import concourse.bass as bass
from concourse import mybir

F32 = mybir.dt.float32
F32R = mybir.dt.float32r
I32 = mybir.dt.int32
U32 = mybir.dt.uint32
ACT = mybir.ActivationFunctionType
ALU = mybir.AluOpType
AX = mybir.AxisListType

P = 128
D = 1024
KD = D // P
SEQ, NB, DS = 1024, 8, 8
NPT = SEQ // P
NT = NPT + 1
TS = NB * DS
N = SEQ + TS
DA, DB, DC = 384, 384, 256
AH, AHD = 4, 96
MEM, XH, XD = 256, 4, 256
MT = MEM // P
NG, EPG = 4, 8
NE = NG * EPG
FE = 256
POOLB = 15
EPS = 1e-6
GT = 3
CHUNKS = [(0, 384), (384, 352), (736, 352)]
SPILL = 2 * N // P - 1
NPLACE = NE * NT
NOWHERE = 1 << 20
LG = 40
NEG = -3.0e38

C_ID, C_UP, C_MASK, C_ONE, C_INV, C_IOTA, C_END = 0, 128, 256, 384, 512, 544, 576
V_GMIX, V_GX, V_GFFN, V_CONV, V_SPOOL, V_BS, V_BS8, V_END = 0, 8, 16, 24, 33, 35, 39, 43
R_LNG, R_LNB, R_BIAS, R_END = 0, DA, 2 * DA, 2 * DA + LG


def rows_of(t):
    return P if t < NPT else TS


def cols_of(t):
    return slice(P * t, P * t + rows_of(t))


def trunk_step(nc, i_, o_):
    ctx = ExitStack()
    with ctx:
        def sb(name, cols, dt=F32, rows=P):
            return ctx.enter_context(nc.sbuf_tensor(name, [rows, cols], dt))

        def sem(name):
            return ctx.enter_context(nc.semaphore(name))

        def v3(buf, c0, a, b):
            return buf[:, c0:c0 + a * b].rearrange("p (a b) -> p a b", a=a)

        def region(name, cols):
            at = (nc.sbuf_base + 31) // 32 * 32
            full_ = sb(name, cols)
            return full_, nc.alloc_sbuf_tensor_at(f"{name}_r", [P, cols], F32R, offset=at)

        regX = sb("regX", NT * D)
        regA, regAr = region("regA", KD * N)
        regB, regBr = region("regB", KD * N)
        regY, regYr = region("regY", KD * N)
        regS, regSr = region("regS", 6144)
        regW, regWr = region("regW", 7680)
        cst = sb("cst", C_END)
        pv = sb("pv", V_END)
        rv = sb("rv", R_END)
        wpool = sb("wpool", 2 * P)
        wst = sb("wst", AH * P)
        wrt = sb("wrt", KD * LG)
        stat = sb("stat", 8 * 40)
        bst = sb("bst", 9 * 8)
        lgm = sb("lgm", NT * LG)
        top = sb("top", NT * 16)
        small = sb("small", 64)
        gate = sb("gate", NT * 8)

        ident = cst[:, C_ID:C_ID + P]
        upper = cst[:, C_UP:C_UP + P]
        mask = cst[:, C_MASK:C_MASK + P]
        ones = cst[:, C_ONE:C_ONE + P]
        invt = v3(cst, C_INV, 2, 16)
        iota = cst[:, C_IOTA:C_IOTA + NE]

        X = v3(regX, 0, NT, D)
        U = v3(regX, 0, NT, DA)
        V = v3(regX, NT * DA, NT, DA)
        xin = v3(regS, 0, 3, D)
        junk1 = regS[:, 3 * D:4 * D]
        diag = v3(regS, 4 * D, 2, P)
        xn2 = v3(regS, 4 * D, 2, D)
        A_hi, Y_f, Y_lo = v3(regAr, 0, KD, N), v3(regY, 0, KD, N), v3(regYr, 0, KD, N)
        B_f, B_lo = v3(regB, 0, KD, N), v3(regBr, 0, KD, N)
        YT = B_f
        LP, LS = POOLB + SEQ, POOLB + DS
        LZ = LP + NB * LS
        pz, pa, pb = (regS[:, k * LZ:k * LZ + LZ] for k in range(3))
        pd = regS[:, 3 * LZ:3 * LZ + N]
        zc = regS[:, 3 * LZ + N:3 * LZ + N + 2 + SEQ]
        zcs = v3(regS, 3 * LZ + N + 2 + SEQ, NB, 2 + DS)
        wsrc = v3(regW, 6144, AH, P)
        w8src = regW[0:TS, 6144 + AH * P:6144 + AH * P + AH * TS].rearrange("p (a b) -> p a b", a=AH)
        spare = regX[:, 2 * NT * DA:NT * D]
        scin = spare[0:16, 0:DB]
        spin = spare[0:NB * POOLB, DB:DB + DC]
        sct = spare[:, 640:640 + 48].rearrange("p (a b) -> p a b", a=3)
        spt = spare[:, 688:688 + 240].rearrange("p (a b) -> p a b", a=2)
        tailb = spare[:, 928:928 + 54].rearrange("p (a b) -> p a b", a=3)
        tailp = spare[:, 982:982 + 158].rearrange("p (a b) -> p a b", a=2)
        outb = spare[0:18, 1140:1140 + DB]
        outp = spare[0:79, 1524:1524 + DC]
        ptmp = spare[:, 1780:1796]
        wst8 = spare[:, 1796:1796 + AH * TS]
        memT = v3(regW, 1024, KD, MEM)
        KT = v3(regS, 0, KD, MEM)
        VP = v3(regS, 2048, MT, D)
        Kn = v3(regY, 6656, MT, D)
        kv_w = [regW[:, 3072:4096] if c == 0 else regY[:, D * ((c - 1) % 3):D * ((c - 1) % 3) + D]
                for c in range(2 * KD)]
        QT = Y_f
        QM = [regS[:, 4096 + 512 * f:4608 + 512 * f] for f in range(4)] + \
            [regW[:, 3072:3584], regW[:, 3584:4096], regW[:, 7168:7680], wst[:, :]]
        KTS = [v3((regA, regB)[c // 3], 2 * N + 2048 * (c % 3), KD, MEM) for c in range(6)]
        PT = [v3(regW, 2048 * k, MT, SEQ) for k in range(2)]
        PR = [v3(regW, 4096 + 512 * k, 2, MEM) for k in range(2)]
        PS = regW[0:TS, 5120:6144].rearrange("p (a b) -> p a b", a=XH)
        ON = regW[0:TS, 6144:7168]
        PTM = regY[:, 4 * N:4 * N + 4096]
        VC = [v3(regS, 4096, MT, D), v3(regY, 0, MT, D), v3(regY, 2 * N, MT, D)]
        YT3 = [v3(regW, 4096 + D * k, KD, P) for k in range(3)]

        chunk_at, chunk_no, chunk_list = {}, {}, {"v": [], "g": []}

        def chunk(key, by, raw, hi, width):
            reg, reg_r, c = raw
            chunk_list[by].append(key)
            chunk_no[key] = (len(chunk_at) + 1, by, len(chunk_list[by]))
            chunk_at[key] = (reg[:, c:c + width], reg_r[:, c:c + width], hi[0][:, hi[1]:hi[1] + width])

        Wp, Sp, Yp, Bp = (regW, regWr), (regS, regSr), (regY, regYr), (regB, regBr)
        for k in range(KD):
            chunk(("U", k), "v", (*Bp, DA * k), (regWr, DA * k), DA)
        for k in range(KD):
            chunk(("V", k), "v", (*Bp, DA * (KD + k)), (regWr, DA * (KD + k)), DA)
        for w in range(11):
            chunk(("F", w), "g", (*Wp, 2048 * (w % 3)), (regWr, 2048 * (w % 3) + D), D)
        for k in range(KD):
            raw = (*Sp, D * k) if k < 4 else (*Wp, (4096, 5120, 6144, 0)[k - 4])
            chunk(("O", k), "v", raw, (regYr, D * k), D)
        for f in range(KD):
            chunk(("Q", f), "g", (*Wp, (4096, 0, 1024)[f % 3]), (regWr, (5120, 6144, 2048)[f % 3]), D)
        for k in range(KD):
            chunk(("XA", k), "v", (*Sp, 512 * k), (regWr, 512 * k), 512)
        for k in range(KD):
            chunk(("XB", k), "g", (*Yp, 512 * k), (regYr, 4 * N + 512 * k), 512)
        RM12 = v3(regS, 0, 2 * NT, NE)
        RM = v3(regS, 576, NT, NE)
        RMA = v3(regS, 864, NT + 1, NE)
        EX = v3(regS, 1184, NT, 2)
        rank_of = v3(regS, 1216, 2 * GT, NE)
        rk, rq, ra, rb, rc = (regS[:, 1420 + 2 * GT * k:1420 + 2 * GT * (k + 1)] for k in range(5))
        ri = regS[:, 1460:1460 + 2 * GT]
        gix = regS[:, 1470:1470 + GT]
        gone = v3(regS, 1480, GT, NG)
        own = v3(regS, 1500, GT, NE)
        esel = v3(regS, 1600, GT, EPG)
        re_ = v3(regS, 2652, 8, NE)
        rq16 = regS[0:1, 2952:2952 + 16 * NE]
        rts = [regS[0:LG, 3500 + P * k:3500 + P * k + P] for k in range(2)]
        pay = sb("pay", NT * 4, I32)
        plc = sb("plc", NT * 2, I32)
        idx = sb("idx", 3 * NE, I32)
        oix = sb("oix", 2, I32)
        spx = sb("spx", 48, I32)
        cni = sb("cni", NE, I32)
        rs = sb("rs", 32)
        ui = sb("ui", 16 * GT, U32)
        gixg = [sb("gixg0", 2, I32), sb("gixg1", 2, I32)]
        gixs = [sb("gixs0", 2, I32), sb("gixs1", 2, I32)]
        W13 = [v3(regW, 0, KD, 2 * FE), v3(regY, 0, KD, 2 * FE)]
        W2 = [v3(regW, 4096, 2, D), v3(regY, 4096, 2, D)]
        w13_flat, w2_flat = [regW[:, 0:4096], regY[:, 0:4096]], [regW[:, 4096:6144], regY[:, 4096:6144]]
        XGT = [v3(regY, 6144 + D * s, KD, P) for s in range(2)]
        XG = [regA[:, D * s:D * s + D] for s in range(2)]
        YO = [regA[:, 2048 + D * s:2048 + D * s + D] for s in range(2)]
        SIL = [regA[:, 4096 + FE * s:4096 + FE * s + FE] for s in range(2)]
        HID = [regA[:, 4608 + FE * s:4608 + FE * s + FE] for s in range(2)]
        HT = [v3(regA, 5120 + FE * s, 2, P) for s in range(2)]
        Y12 = [v3(regB, 0, 2, D), v3(regB, 2 * D, 2, D), v3(regA, 0, 2, D)]
        FO = [regB[:, 4 * D + D * s:5 * D + D * s] for s in range(2)]
        gfin = regB[:, 6 * D:7 * D]
        junk = regB[:, 7 * D:8 * D]

        table = nc.dram_tensor("place_table", [P * NPLACE, 2], I32, kind="Internal").ap()
        xn_dram = nc.dram_tensor("normed_tokens", [N, D], F32, kind="Internal").ap()
        y_dram = nc.dram_tensor("expert_rows", [2 * N, D], F32, kind="Internal").ap()

        bank = [ctx.enter_context(nc.psum_tensor(f"bank{b}", [P, 512], F32)) for b in range(8)]

        full = [sem(f"full{b}") for b in range(8)]
        drained = [sem(f"drained{b}") for b in range(8)]
        uses = [0] * 8
        use_of = {}

        def take(key, b):
            assert key not in use_of
            if uses[b]:
                nc.tensor.wait_ge(drained[b], uses[b])
            uses[b] += 1
            use_of[key] = (b, uses[b])
            return bank[b]

        def filled(eng, key):
            b, n = use_of[key]
            eng.wait_ge(full[b], n)
            return bank[b], drained[b]

        def emptied(eng, key):
            b, n = use_of[key]
            eng.wait_ge(drained[b], n)

        w_hi, w_lo = sem("w_hi"), {"v": sem("w_lo_v"), "g": sem("w_lo_g")}
        x_hi, x_lo = [sem(f"x_hi{k}") for k in range(3)], [sem(f"x_lo{k}") for k in range(4)]

        def hi_of(act, key):
            raw, _, hi = chunk_at[key]
            nc.scalar.activation(hi, raw, ACT.Copy).then_inc(w_hi, 1)

        def lo_of(eng, name, key):
            raw, lo, hi = chunk_at[key]
            eng.wait_ge(w_hi, chunk_no[key][0])
            eng.tensor_tensor(lo, raw, hi.bitcast(F32), ALU.subtract).then_inc(w_lo[name], 1)

        def chunk_ready(key):
            _, by, n = chunk_no[key]
            nc.tensor.wait_ge(w_lo[by], n)
            return chunk_at[key][2], chunk_at[key][1]

        s_cst = sem("s_cst")
        s_x = [sem(f"s_x{k}") for k in range(3)]
        s_wu = [sem(f"s_wu{k}") for k in range(4)]
        s_wv = sem("s_wv")
        s_ws = [sem(f"s_ws{k}") for k in range(3)]
        s_wo = [sem(f"s_wo{k}") for k in range(3)]
        s_wx = sem("s_wx")
        s_kvw = [sem(f"s_kvw{k}") for k in range(4)]
        s_kvd = sem("s_kvd")
        s_xg = sem("s_xg")
        s_xs = sem("s_xs")
        s_dg = sem("s_dg")
        s_oh = sem("s_oh")
        s_kd = sem("s_kd")
        s_vfree = sem("s_vfree")
        s_wst = sem("s_wst")
        s_rv = sem("s_rv")
        s_xr = [sem(f"s_xr{t}") for t in range(3)]
        s_kc = [sem(f"s_kc{k}") for k in range(3)]
        s_vc = [sem(f"s_vc{k}") for k in range(3)]
        s_sq = [sem(f"s_sq{k}") for k in range(4)]
        s_rt = [sem(f"s_rt{k}") for k in range(4)]
        s_xn = [None, None, sem("s_xn2"), sem("s_xn3")]
        s_bn = sem("s_bn")
        s_lrt = sem("s_lrt")
        s_vln = sem("s_vln")
        s_zero = sem("s_zero")
        s_tail = sem("s_tail")
        s_pd = sem("s_pd")
        s_mxs = sem("s_mxs")
        s_pns = sem("s_pns")
        s_outs = sem("s_outs")
        s_kout = sem("s_kout")
        s_mx = sem("s_mx")
        s_pn = sem("s_pn")
        s_qz = sem("s_qz")
        s_qm = sem("s_qm")
        s_rma = sem("s_rma")
        s_xnd = [sem("s_xnd0"), sem("s_xnd1")]
        s_pre = sem("s_pre")
        s_plc = sem("s_plc")
        s_ug = sem("s_ug")
        s_scat = sem("s_scat")
        s_idx = sem("s_idx")
        s_gd = sem("s_gd")
        s_ge = sem("s_ge")
        s_dv = sem("s_dv")
        s_waited = sem("s_waited")
        m_gi = [sem("m_gi0"), sem("m_gi1")]
        m_si = [sem("m_si0"), sem("m_si1")]
        m_w = [sem("m_w0"), sem("m_w1")]
        m_w2 = [sem("m_w20"), sem("m_w21")]
        m_g = [sem("m_g0"), sem("m_g1")]
        m_tx = [sem("m_tx0"), sem("m_tx1")]
        m_xt = [sem("m_xt0"), sem("m_xt1")]
        m_ab = [sem("m_ab0"), sem("m_ab1")]
        m_sil = [sem("m_sil0"), sem("m_sil1")]
        m_hid = [sem("m_hid0"), sem("m_hid1")]
        m_th = [sem("m_th0"), sem("m_th1")]
        m_ht = [sem("m_ht0"), sem("m_ht1")]
        m_y = [sem("m_y0"), sem("m_y1")]
        m_yo0 = [sem("m_yo00"), sem("m_yo01")]
        m_yo1 = [sem("m_yo10"), sem("m_yo11")]
        m_sc = [sem("m_sc0"), sem("m_sc1")]
        o_go = sem("o_go")
        o_w = sem("o_w")
        o_ix = sem("o_ix")
        o_g = sem("o_g")
        o_tx = sem("o_tx")
        o_xt = sem("o_xt")
        o_ab = sem("o_ab")
        o_sil = sem("o_sil")
        o_hid = sem("o_hid")
        o_th = sem("o_th")
        o_ht = sem("o_ht")
        o_y = sem("o_y")
        o_yo = sem("o_yo")
        o_sc = sem("o_sc")
        s_moe = sem("s_moe")
        s_gf = sem("s_gf")
        s_fadd = sem("s_fadd")
        s_fo = sem("s_fo")
        s_fst = [sem("s_fst0"), sem("s_fst1")]

        block = ctx.enter_context(nc.Block())

        B_AB, B_TX, B_TH, B_Y = [0, 1], [2, 3], 4, [5, 6]

        @block.tensor
        def _(pe):
            def mm_group(out, pairs, signal=None):
                for k, (lhsT, rhs) in enumerate(pairs):
                    last = nc.tensor.matmul(out, lhsT, rhs, start=(k == 0), stop=(k == len(pairs) - 1))
                if signal is not None:
                    last.then_inc(signal, 1)

            def transposes(key, b, parts):
                ps = take(key, b)
                for src, c in parts:
                    r, m = src.shape[0], src.shape[-1]
                    last = nc.tensor.transpose(ps[0:m, c:c + r], src, ident[0:r, 0:r])
                last.then_inc(full[b], 1)

            def tx_norm(s, t):
                r = rows_of(t)
                pe.wait_ge(s_xn[s], t + 1)
                for q in range(2):
                    transposes(("T", s, t, q), 6 + q,
                               [(xn2[0:r, t % 2, P * (4 * q + k):P * (4 * q + k + 1)], P * k) for k in range(4)])

            def product(out, stays, moves, first, last, signal=None):
                nc.tensor.matmul(out, stays[0], moves[1], start=first, stop=False)
                nc.tensor.matmul(out, stays[1], moves[0], start=False, stop=False)
                ins = nc.tensor.matmul(out, stays[0], moves[0], start=False, stop=last)
                if signal is not None:
                    ins.then_inc(signal, 1)

            def scale(t):
                r = rows_of(t)
                pe.wait_ge(s_dg, t + 1)
                ps = take(("N1", t), 6 + t % 2)
                nc.tensor.matmul(ps[:, 0:r], ones[0:r, :], diag[0:r, t % 2, 0:r],
                                 start=True, stop=True).then_inc(full[6 + t % 2], 1)

            pe.wait_ge(s_cst, 32)
            scale(0)
            for which, name in enumerate("UV"):
                for t in range(NT):
                    if name == "U" and 0 < t < NT - 1:
                        scale(t + 1)
                    r = rows_of(t)
                    pe.wait_ge(x_lo[1], t + 1)
                    b = 3 * which + t % 3
                    ps = take((name, t), b)
                    for k in range(KD):
                        if name == "U" and t == 0 and k == 4:
                            scale(1)
                        product(ps[0:r, 0:DA], (A_hi[:, k, cols_of(t)], Y_lo[:, k, cols_of(t)]),
                                chunk_ready((name, k)), k == 0, k == KD - 1, full[b] if k == KD - 1 else None)
            pe.wait_ge(s_wst, 64)
            transposes(("WS",), 4, [(wsrc[:, h, :], P * h) for h in range(AH)])
            transposes(("W8",), 5, [(w8src[:, h, :], TS * h) for h in range(AH)])
            transposes(("SC",), 4, [(scin[:, P * j:P * j + P], 16 * j) for j in range(3)])
            transposes(("SP",), 5, [(spin[:, P * j:P * j + P], 120 * j) for j in range(2)])

            ring = 0

            def bc_tile(name, j, w):
                nonlocal ring
                wt = [x.rearrange("p (k n) -> p k n", k=KD) for x in chunk_ready(("F", w))]
                for c, (c0, cn) in enumerate(CHUNKS):
                    b = ring % 6
                    ring += 1
                    ps = take((name, j, c), b)
                    for k in range(KD):
                        product(ps[:, 0:cn], (wt[0][:, k, :], wt[1][:, k, :]),
                                (A_hi[:, k, c0:c0 + cn], Y_lo[:, k, c0:c0 + cn]),
                                k == 0, k == KD - 1, full[b] if k == KD - 1 else None)

            def pooled(j):
                nonlocal ring
                pe.wait_ge(s_rv, 48)
                pe.wait_ge(s_pd, j + 1)
                for c, (c0, cn) in enumerate(CHUNKS):
                    b = ring % 6
                    ring += 1
                    ps = take(("P", j, c), b)
                    mm_group(ps[:, 0:cn], [(wpool[:, P * j:P * j + P], pd[:, c0:c0 + cn])], full[b])

            def chunk_gate(g, h):
                t0, n = (4 * g, 4) if g < 2 else (NPT, 1)
                r = rows_of(t0)
                pe.wait_ge(s_vln, t0 + n)
                emptied(pe, ("WS",) if g < 2 else ("W8",))
                ps = take(("G", g, h), 6 + h % 2)
                w = v3(wst, 0, AH, P)[:, h, :] if g < 2 else wst8[0:TS, TS * h:TS * h + TS]
                nc.tensor.matmul(ps[0:r, 0:n * AHD].rearrange("p (t d) -> p t d", t=n), w,
                                 V[0:r, t0:t0 + n, AHD * h:AHD * h + AHD],
                                 start=True, stop=True).then_inc(full[6 + h % 2], 1)

            def gated_turn(t):
                r = rows_of(t)
                for h in range(AH):
                    emptied(pe, ("G", t // 4, h))
                transposes(("Y", t), t % 2, [(U[0:r, t, P * k:P * k + P], P * k) for k in range(3)])

            bc_tile("Z", 0, 0)
            bc_tile("Z", 1, 1)
            for part, name in enumerate("CXB"):
                bc_tile(name, 0, 2 + part)
            pooled(0)
            for part, name in enumerate("CXB"):
                bc_tile(name, 1, 5 + part)
                for h in range(AH):
                    chunk_gate(part, h)
            pooled(1)
            for t in range(NT):
                gated_turn(t)
            for part, name in enumerate("CXB"):
                bc_tile(name, 2, 8 + part)
            pe.wait_ge(s_tail, 3)
            transposes(("TB",), 6, [(tailb[:, j, :], P * j) for j in range(3)])
            transposes(("TP",), 7, [(tailp[:, j, :], P * j) for j in range(2)])

            for t in range(NT + 1):
                if t < NT:
                    r = rows_of(t)
                    pe.wait_ge(x_lo[0], t + 1)
                    ps = [take(("O1", t, h), 2 * (t % 2) + h) for h in range(2)]
                    for k in range(KD):
                        hi, lo = chunk_ready(("O", k))
                        for h in range(2):
                            product(ps[h][0:r, :], (A_hi[:, k, cols_of(t)], B_lo[:, k, cols_of(t)]),
                                    (hi[:, 512 * h:512 * h + 512], lo[:, 512 * h:512 * h + 512]),
                                    k == 0, k == KD - 1, full[2 * (t % 2) + h] if k == KD - 1 else None)
                if 0 < t < NT:
                    tx_norm(2, t - 1)
            for which, name in enumerate("KV"):
                ps = {(m, h): take((name, m, h), 4 * which + 2 * m + h) for m in range(MT) for h in range(2)}
                for k in range(KD):
                    c = KD * which + k
                    pe.wait_ge(s_kvw[0 if c == 0 else 1 + (c - 1) % 3], 32 if c == 0 else 16 * ((c - 1) // 3 + 1))
                    for m in range(MT):
                        for h in range(2):
                            ins = nc.tensor.matmul(ps[m, h][:, :], memT[:, k, P * m:P * m + P],
                                                   kv_w[c][:, 512 * h:512 * h + 512],
                                                   start=(k == 0), stop=(k == KD - 1))
                            if k == KD - 1:
                                ins.then_inc(full[4 * which + 2 * m + h], 1)
                    if k < KD - 1:
                        ins.then_inc(s_kvd, 1)
                    if c == 1:
                        tx_norm(2, NT - 1)
            for q in range(4):
                for m in range(MT):
                    emptied(pe, ("K", m, q // 2))
                transposes(("TK", q), q,
                           [(Kn[:, m, P * (2 * q + k):P * (2 * q + k) + P], MEM * k + P * m)
                            for k in range(2) for m in range(MT)])
            def scores(n):
                h, tp = n // 4, n % 4
                for c in range(3):
                    emptied(pe, ("Q", 2 * h + 1, c))
                if n == 0:
                    emptied(pe, ("TK", 2))
                    emptied(pe, ("TK", 3))
                b = n % 3
                ps = take(("S", n), b)
                for a in range(2):
                    t = 2 * tp + a
                    for k in range(2):
                        last = nc.tensor.matmul(ps[:, MEM * a:MEM * a + MEM],
                                                QT[:, 2 * h + k, P * t:P * t + P], KT[:, 2 * h + k, :],
                                                start=(k == 0), stop=(k == 1))
                last.then_inc(full[b], 1)

            pe.wait_ge(x_lo[2], NT)
            ring = 0
            for f in range(KD):
                if f == KD - 2:
                    scores(0)
                    scores(1)
                wt = [x.rearrange("p (k n) -> p k n", k=KD) for x in chunk_ready(("Q", f))]
                for c, (c0, cn) in enumerate(CHUNKS):
                    b = 4 + ring % 4
                    ring += 1
                    ps = take(("Q", f, c), b)
                    for k in range(KD):
                        product(ps[:, 0:cn], (wt[0][:, k, :], wt[1][:, k, :]),
                                (A_hi[:, k, c0:c0 + cn], B_lo[:, k, c0:c0 + cn]),
                                k == 0, k == KD - 1, full[b] if k == KD - 1 else None)

            def turn(n):
                pe.wait_ge(s_pn, n + 1)
                pr = PR[n % 2]
                transposes(("PT", n), 3, [(pr[:, a, P * m:P * m + P], MEM * m + P * a)
                                          for m in range(MT) for a in range(2)])

            def values(h):
                emptied(pe, ("PT", 4 * h + 3))
                if h == 0:
                    emptied(pe, ("V", 0, 1))
                    emptied(pe, ("V", 1, 1))
                for e in range(2):
                    for c in range(2):
                        b = 4 + 2 * e + c
                        ps = take(("PV", h, e, c), b)
                        mm_group(ps[:, :], [(VP[:, m, XD * h + P * e:XD * h + P * e + P],
                                             PT[h % 2][:, m, 512 * c:512 * c + 512]) for m in range(MT)], full[b])

            def sample_scores():
                pe.wait_ge(s_qm, KD)
                ps_h = [take(("SS", h), 4 + h) for h in range(XH)]
                for b_ in range(NB):
                    pe.wait_ge(s_kc[b_ // 2 % 3], 32 * (b_ // 6 + 1))
                    for h in range(XH):
                        for k in range(2):
                            f = 2 * h + k
                            last = nc.tensor.matmul(ps_h[h][0:TS, 0:MEM], QM[f][:, TS * b_:TS * b_ + TS],
                                                    KTS[b_ % 6][:, f, :],
                                                    start=(b_ == 0 and k == 0), stop=(b_ == NB - 1 and k == 1))
                        if b_ == NB - 1:
                            last.then_inc(full[4 + h], 1)
                        elif h == XH - 1:
                            last.then_inc(s_kd, 1)

            for n in range(16):
                if n + 2 < 16:
                    scores(n + 2)
                if n == 4:
                    values(0)
                    sample_scores()
                turn(n)
                if n % 4 == 0 and n > 4:
                    values(n // 4 - 1)
            values(3)

            pe.wait_ge(s_pns, 1)
            transposes(("PTS",), 3, [(PS[:, h, P * m:P * m + P], TS * (MT * h + m))
                                     for h in range(XH) for m in range(MT)])
            emptied(pe, ("PTS",))
            sample_bank = [0, 1, 2, 3]
            ps_h = [take(("PVS", h), sample_bank[h]) for h in range(XH)]
            for b_ in range(NB):
                pe.wait_ge(s_vc[b_ % 3], 16 * (b_ // 3 + 1))
                for h in range(XH):
                    for m in range(MT):
                        g = MT * h + m
                        last = nc.tensor.matmul(ps_h[h][0:TS, 0:XD],
                                                PTM[:, 512 * g + TS * b_:512 * g + TS * b_ + TS],
                                                VC[b_ % 3][:, m, XD * h:XD * h + XD],
                                                start=(b_ == 0 and m == 0), stop=(b_ == NB - 1 and m == 1))
                    if b_ == NB - 1:
                        last.then_inc(full[sample_bank[h]], 1)
                    elif h == XH - 1:
                        last.then_inc(s_vfree, 1)

            def out_half(t, h):
                r = rows_of(t)
                pe.wait_ge(x_lo[3], 16 if t < NPT else 17)
                b = 4 + t % 2 if h == 0 else 1 + 2 * (t % 2)
                ps = take(("O2", t, h), b)
                for k in range(KD):
                    product(ps[0:r, :], (A_hi[:, k, cols_of(t)], B_lo[:, k, cols_of(t)]),
                            chunk_ready(("XB" if h else "XA", k)), k == 0, k == KD - 1,
                            full[b] if k == KD - 1 else None)

            for t in range(NT):
                out_half(t, 0)
                if t == 0:
                    for h in range(XH):
                        emptied(pe, ("PVS", h))
                    transposes(("TO",), 6, [(ON[:, P * k:P * k + P], TS * k) for k in range(KD)])
            wr = v3(wrt, 0, KD, LG)

            def router(t):
                r = rows_of(t)
                emptied(pe, ("T", 3, t, 0))
                emptied(pe, ("T", 3, t, 1))
                ps = take(("R", t), 4)
                mm_group(ps[0:LG, 0:r], [(wr[:, k, :], YT3[t % 3][:, k, 0:r]) for k in range(KD)], full[4])

            def logits(t):
                emptied(pe, ("R", t))
                transposes(("L", t), 5, [(rts[t % 2][:, 0:rows_of(t)], 0)])

            def ranks(b_):
                ps = take(("RK", b_), 0)
                for j in range(GT):
                    t = GT * b_ + j
                    pe.wait_ge(s_rma, t + 1)
                    mm_group(ps[:, NE * j:NE * j + NE], [(upper, RM[:, t, :]), (ones, RMA[:, t, :])],
                             full[0] if j == GT - 1 else None)

            for t in range(NT + 4):
                if t < NT:
                    out_half(t, 1)
                if 0 <= t - 1 < NT:
                    tx_norm(3, t - 1)
                if 0 <= t - 2 < NT:
                    router(t - 2)
                if 0 <= t - 3 < NT:
                    logits(t - 3)
                if t >= 6 and t % GT == 0:
                    ranks(t // GT - 2)
            ps = take(("CN",), 2)
            mm_group(ps[:, 0:NE], [(ones, RMA[:, NT, :])], full[2])

            def tx(s, signal):
                for q in range(2):
                    for k in range(4):
                        last = nc.tensor.transpose(bank[B_TX[q]][:, P * k:P * k + P],
                                                   XG[s][:, P * (4 * q + k):P * (4 * q + k) + P], ident)
                last.then_inc(signal, 1)

            def ab(s, signal, b):
                mm_group(bank[b][:, :], [(XGT[s][:, k, :], W13[s][:, k, :]) for k in range(KD)], signal)

            def th(s, signal):
                for k in range(2):
                    last = nc.tensor.transpose(bank[B_TH][:, P * k:P * k + P], HID[s][:, P * k:P * k + P], ident)
                last.then_inc(signal, 1)

            def yy(s, signal):
                for h in range(2):
                    mm_group(bank[B_Y[h]][:, :], [(HT[s][:, k, :], W2[s][:, k, 512 * h:512 * h + 512])
                                                  for k in range(2)], signal if h else None)

            for b in range(8):
                pe.wait_ge(drained[b], uses[b])
            pe.wait_ge(m_g[0], 16)
            tx(0, m_tx[0])
            pe.wait_ge(m_w[0], 16)
            pe.wait_ge(m_xt[0], 1)
            ab(0, m_ab[0], B_AB[0])
            pe.wait_ge(m_g[1], 16)
            tx(1, m_tx[1])
            with pe.Fori(0, NE // 2 - 1) as i:
                for e0, s in ((1, 1), (2, 0)):
                    q = 1 - s
                    n = i + 1 if s else i + 2
                    nq = i + 1
                    pe.wait_ge(m_w[s], 16 * n)
                    pe.wait_ge(m_xt[s], n)
                    ab(s, m_ab[s], B_AB[s])
                    pe.wait_ge(m_hid[q], nq)
                    th(q, m_th[q])
                    pe.wait_ge(m_g[q], 16 * (nq + 1))
                    tx(q, m_tx[q])
                    pe.wait_ge(m_w2[q], 16 * nq)
                    pe.wait_ge(m_ht[q], nq)
                    pe.wait_ge(m_yo0[s], nq)
                    pe.wait_ge(m_yo1[s], nq)
                    yy(q, m_y[q])
            NH = NE // 2
            pe.wait_ge(m_w[1], 16 * NH)
            pe.wait_ge(m_xt[1], NH)
            ab(1, m_ab[1], B_AB[1])
            pe.wait_ge(m_hid[0], NH)
            th(0, m_th[0])
            pe.wait_ge(m_w2[0], 16 * NH)
            pe.wait_ge(m_ht[0], NH)
            pe.wait_ge(m_yo0[1], NH)
            pe.wait_ge(m_yo1[1], NH)
            yy(0, m_y[0])
            pe.wait_ge(m_hid[1], NH)
            th(1, m_th[1])
            pe.wait_ge(m_w2[1], 16 * NH)
            pe.wait_ge(m_ht[1], NH)
            pe.wait_ge(m_yo0[0], NH)
            pe.wait_ge(m_yo1[0], NH)
            yy(1, m_y[1])
            pe.wait_ge(o_go, 1)
            n_spill = pe.value_load(spx[0:1, 16:17], min_val=0, max_val=SPILL)
            with pe.If(n_spill > 0):
                with pe.Fori(0, SPILL) as q:
                    pe.wait_ge(o_g, 16 * q + 16)
                    tx(0, o_tx)
                    pe.wait_ge(o_w, 16 * q + 16)
                    pe.wait_ge(o_xt, q + 1)
                    ab(0, o_ab, B_AB[0])
                    pe.wait_ge(o_hid, q + 1)
                    th(0, o_th)
                    pe.wait_ge(o_ht, q + 1)
                    pe.wait_ge(o_yo, 2 * q + 1)
                    yy(0, o_y)

        @block.sync
        def _(sp):
            def load(dst, src, signal):
                sp.dma_start(dst, src).then_inc(signal, 16)

            def x_rows(t):
                return i_["x_prompt"][0, P * t:P * t + P, :] if t < NPT else \
                    i_["x_sample"].rearrange("b s d -> (b s) d")

            def x_of(t):
                if t >= 3:
                    sp.wait_ge(s_sq[1], t - 2)
                load(xin[0:rows_of(t), t % 3], x_rows(t), s_x[t % 3])
                load(Y_f[:, :, cols_of(t)], i_["xt"][:, :, cols_of(t)], s_x[t % 3])

            load(xin[:, 0], x_rows(0), s_x[0])
            load(cst[:, :], i_["cst"], s_cst)
            load(pv[:, :], i_["pv"], s_cst)
            load(Y_f[:, :, 0:P], i_["xt"][:, :, 0:P], s_x[0])
            for q in range(4):
                c = 2 * DA * q
                load(regB[:, c:c + 2 * DA], i_["wu"][:, c:c + 2 * DA], s_wu[q])
            for t in range(1, NT):
                x_of(t)
                if t == 3:
                    load(regB[:, KD * DA:2 * KD * DA], i_["wv"], s_wv)
                if t == 4:
                    load(wpool[:, :], i_["wpool"], s_rv)
                    load(rv[:, :], i_["rv"], s_rv)
                    load(wsrc, i_["ws"], s_wst)
                    load(w8src, i_["w8"], s_wst)
                    load(scin, i_["state_conv"][0].rearrange("b r d -> (b r) d"), s_wst)
                    load(spin, i_["state_pool"][0].rearrange("b r d -> (b r) d"), s_wst)
                    load(wrt[:, :], i_["wr"], s_rv)
            names = [("Z", 0), ("Z", 1)] + [(c, j) for j in range(3) for c in "CXB"]
            for w in range(11):
                if w < 3:
                    filled(sp, ("V" if w else "U", NT - 1))
                else:
                    filled(sp, (*names[w - 3], 2))
                load(chunk_at["F", w][0], i_["wbc"][w], s_ws[w % 3])

            def o_load(k):
                load(chunk_at["O", k][0], i_["wo"][:, D * k:D * k + D], s_wo[0 if k < 4 else 1 if k < 7 else 2])

            filled(sp, ("P", 1, 2))
            for k in range(4):
                o_load(k)
            filled(sp, ("C", 2, 2))
            for k in range(4, 7):
                o_load(k)
            filled(sp, ("X", 2, 2))
            o_load(7)
            for c in range(3):
                filled(sp, ("B", 2, c))
            load(memT, i_["memt"], s_kvw[0])
            load(kv_w[0], i_["wk"][:, 0:D], s_kvw[0])
            filled(sp, ("TP",))
            sp.wait_ge(s_outs, 16 * 6)
            for t in range(NT):
                load(X[0:rows_of(t), t], x_rows(t), s_xr[t // 3])
            filled(sp, ("O1", NT - 1, 1))

            def kv_load(c):
                if c >= 4:
                    if c - 3 < KD - 1:
                        sp.wait_ge(s_kvd, c - 2)
                    elif c - 3 == KD - 1:
                        filled(sp, ("K", 1, 1))
                    else:
                        sp.wait_ge(s_kvd, c - 3)
                load(kv_w[c], i_["wk" if c < KD else "wvx"][:, D * (c % KD):D * (c % KD) + D],
                     s_kvw[1 + (c - 1) % 3])

            def q_load(f):
                load(chunk_at["Q", f][0], i_["wq"][f], s_ws[f % 3])

            for c in range(1, 4):
                kv_load(c)
            q_load(0)
            q_load(1)
            for c in range(4, 2 * KD):
                kv_load(c)
            for m in range(MT):
                for h in range(2):
                    filled(sp, ("V", m, h))
            q_load(2)
            for f in range(3, KD):
                filled(sp, ("Q", f - 3, 2))
                q_load(f)
            for c in range(3):
                filled(sp, ("Q", KD - 1, c))
            for b_ in range(NB):
                if b_ >= 6:
                    sp.wait_ge(s_kd, b_ - 5)
                load(KTS[b_ % 6], i_["kct"][b_], s_kc[b_ // 2 % 3])

            def value_load(b_):
                load(VC[b_ % 3], i_["cache_mem_v"][0, b_].rearrange("(m p) h e -> p m (h e)", p=P), s_vc[b_ % 3])

            for h in range(XH):
                filled(sp, ("SS", h))
            value_load(0)
            value_load(1)
            filled(sp, ("S", 7))
            value_load(2)
            for e in range(2):
                for c in range(2):
                    filled(sp, ("PV", XH - 1, e, c))
            wxo = i_["wxo"].rearrange("p (k n) -> p k n", k=KD)
            for b_ in range(3, NB):
                sp.wait_ge(s_vfree, b_ - 2)
                value_load(b_)
                if b_ in (3, 4):
                    k = 4 * (b_ - 3)
                    load(v3(regS, 512 * k, 4, 512), wxo[:, k:k + 4, 0:512], s_wx)
            for h in range(XH):
                filled(sp, ("PVS", h))
            load(v3(regY, 0, KD, 512), wxo[:, :, 512:D], s_wx)
            filled(sp, ("O2", NT - 1, 0))
            load(w13_flat[0], i_["we"][0, :, 0:4096], m_w[0])
            for t in range(NT):
                sp.wait_ge(s_xn[3], t + 1)
                load(xn_dram[P * t:P * t + rows_of(t), :], xn2[0:rows_of(t), t % 2], s_xnd[t % 2])
            filled(sp, ("O2", NT - 1, 1))
            load(w13_flat[1], i_["we"][1, :, 0:4096], m_w[1])
            load(w2_flat[1], i_["we"][1, :, 4096:6144], m_w2[1])
            filled(sp, ("R", NT - 1))
            load(w2_flat[0], i_["we"][0, :, 4096:6144], m_w2[0])
            sp.wait_ge(s_scat, 16 * 2 * NT)
            load(v3(idx, 0, NE, 2), table.rearrange("(p c) k -> p c k", p=P)[:, 0:NE, :], s_idx)

            def weights(dst, e, c0, c1, signal):
                sp.dma_start(dst, i_["we"][bass.ds(e, 1), :, c0:c1].rearrange("a p n -> (a p) n")) \
                    .then_inc(signal, 16)

            sp.wait_ge(m_ab[0], 1)
            load(w13_flat[0], i_["we"][2, :, 0:4096], m_w[0])
            with sp.Fori(0, NE // 2 - 2) as i:
                for e0, s in ((1, 1), (2, 0)):
                    sp.wait_ge(m_ab[s], i + e0)
                    weights(w13_flat[s], 2 * i + e0 + 2, 0, 4096, m_w[s])
                    sp.wait_ge(m_y[1 - s], i + 1)
                    weights(w2_flat[1 - s], 2 * i + e0 + 1, 4096, 6144, m_w2[1 - s])
            NH = NE // 2
            sp.wait_ge(m_ab[1], NH - 1)
            load(w13_flat[1], i_["we"][NE - 1, :, 0:4096], m_w[1])
            for s in range(2):
                sp.wait_ge(m_y[s], NH - 1)
                load(w2_flat[s], i_["we"][NE - 2 + s, :, 4096:6144], m_w2[s])
            sp.wait_ge(o_go, 1)
            n_spill = sp.value_load(spx[0:1, 16:17], min_val=0, max_val=SPILL)
            with sp.If(n_spill > 0):
                with sp.Fori(0, SPILL) as q:
                    sp.wait_ge(o_y, q + 1)
                    e = sp.value_load(spx[0:1, bass.ds(q, 1)], min_val=0, max_val=NE - 1)
                    sp.dma_start(regW[:, 0:6144],
                                 i_["we"][bass.ds(e, 1), :, :].rearrange("a p n -> (a p) n")).then_inc(o_w, 16)
                    sp.wait_ge(o_sc, 16 * q + 16)
                    c = sp.value_load(spx[0:1, bass.ds(q + 32, 1)], min_val=0, max_val=NPLACE - 1)
                    sp.dma_start(oix[:, :], table.rearrange("(p c) k -> c p k", p=P)[bass.ds(c, 1), :, :]
                                 .rearrange("a p k -> (a p) k")).then_inc(o_ix, 16)
            sp.wait_ge(s_moe, 1)
            load(gfin, i_["gfin"], s_gf)
            for t in range(NT):
                r = rows_of(t)
                if t >= 3:
                    sp.wait_ge(s_fadd, t - 2)
                for k in range(2):
                    load(Y12[t % 3][0:r, k, :], y_dram[N * k + P * t:N * k + P * t + r, :], s_xr[t % 3])

        @block.scalar
        def _(act):
            def copy(out, in_, signal):
                nc.scalar.activation(out, in_, ACT.Copy).then_inc(signal, 1)

            def norm_act(s, t, src):
                r = rows_of(t)
                c = 40 * s + t
                dst = junk if s == 0 else junk1 if s == 1 else xn2[:, t % 2]
                if s == 1 and t > 0:
                    act.wait_ge(s_sq[1], t)
                nc.scalar.activation(dst[0:r, :], src[0:r], ACT.Square,
                                     accum_out=stat[0:r, c:c + 1]).then_inc(s_sq[s], 1)
                act.wait_ge(s_sq[s], t + 1)
                nc.scalar.activation(stat[0:r, c + 10:c + 11], stat[0:r, c:c + 1], ACT.Sqrt,
                                     scale=1.0 / D, bias=small[0:r, 0:1]).then_inc(s_rt[s], 1)

            act.wait_ge(s_zero, 1)
            def norm_1(t):
                act.wait_ge(s_x[t % 3], 32 * (t // 3 + 1))
                norm_act(1, t, xin[:, t % 3])

            def tokens_hi(stage, t, src):
                nc.scalar.activation(A_hi[:, :, cols_of(t)], src[:, :, cols_of(t)], ACT.Copy).then_inc(x_hi[stage], 1)

            def gelu(name, dst, t):
                r = rows_of(t)
                ps, sg = filled(act, (name, t))
                nc.scalar.activation(dst[0:r, t, :], ps[0:r, 0:DA], ACT.Gelu_apprx_tanh).then_inc(sg, 1)

            nc.scalar.activation(small[:, 1:2], small[:, 0:1], ACT.Sqrt)
            norm_1(0)
            act.wait_ge(s_wu[0], 16)
            hi_of(act, ("U", 0))
            hi_of(act, ("U", 1))
            act.wait_ge(s_xs, 1)
            tokens_hi(1, 0, Y_f)
            norm_1(1)
            for k in range(2, KD):
                act.wait_ge(s_wu[k // 2], 16)
                hi_of(act, ("U", k))
            norm_1(2)
            for t in range(1, NT):
                if t + 2 < NT:
                    norm_1(t + 2)
                if t >= 4:
                    act.wait_ge(s_wv, 16)
                    for k in range(2 * (t - 4), min(2 * (t - 3), KD)):
                        hi_of(act, ("V", k))
                act.wait_ge(s_xs, t + 1)
                tokens_hi(1, t, Y_f)
                ps, sg = filled(act, ("U", t - 1))
                copy(U[:, t - 1, :], ps[:, 0:DA], sg)
            ps, sg = filled(act, ("U", NT - 1))
            copy(U[0:TS, NT - 1, :], ps[0:TS, 0:DA], sg)

            def columns_hi(w):
                act.wait_ge(s_ws[w % 3], 16 * (w // 3 + 1))
                hi_of(act, ("F", w))

            columns_hi(0)
            for t in range(NT):
                gelu("V", V, t)
                emptied(act, ("U", t))
                u = U[0:rows_of(t), t, :]
                nc.scalar.activation(u, u, ACT.Gelu_apprx_tanh).then_inc(s_ug, 1)
            act.wait_ge(s_bn, NT + 1)
            nc.scalar.activation(bst[:, 27:36], bst[:, 18:27], ACT.Sqrt).then_inc(s_lrt, 1)

            def z_copies(j):
                for c, (c0, cn) in enumerate(CHUNKS):
                    ps, sg = filled(act, ("Z", j, c))
                    if j == 1:
                        act.wait_ge(s_pd, 1)
                    if c < 2:
                        copy(pz[:, POOLB + c0:POOLB + c0 + cn], ps[:, 0:cn], sg)
                    else:
                        n = SEQ - c0
                        nc.scalar.activation(pz[:, POOLB + c0:POOLB + SEQ], ps[:, 0:n], ACT.Copy)
                        pzs = pz[:, LP:LZ].rearrange("p (b l) -> p b l", b=NB)
                        copy(pzs[:, :, POOLB:], ps[:, n:cn].rearrange("p (b l) -> p b l", b=NB), sg)

            def c_copies(j):
                for c, (c0, cn) in enumerate(CHUNKS):
                    ps, sg = filled(act, ("C", j, c))
                    if j > 0:
                        act.wait_ge(s_tail, j)
                    n = min(cn, SEQ - c0)
                    ins = nc.scalar.activation(zc[:, 2 + c0:2 + c0 + n], ps[:, 0:n], ACT.Copy)
                    if c == 2:
                        ins = nc.scalar.activation(zcs[:, :, 2:], ps[:, n:cn].rearrange("p (b l) -> p b l", b=NB),
                                                   ACT.Copy)
                    ins.then_inc(sg, 1)

            def p_copies(j):
                for c, (c0, cn) in enumerate(CHUNKS):
                    ps, sg = filled(act, ("P", j, c))
                    nc.scalar.activation(YT[:, 6 + j, c0:c0 + cn], ps[:, 0:cn], ACT.Copy,
                                         scale=pv[:, V_SPOOL + j:V_SPOOL + j + 1]).then_inc(sg, 1)

            columns_hi(1)
            columns_hi(2)
            z_copies(0)
            columns_hi(3)
            z_copies(1)
            columns_hi(4)
            c_copies(0)
            columns_hi(5)
            columns_hi(6)
            columns_hi(7)
            p_copies(0)
            c_copies(1)
            columns_hi(8)
            columns_hi(9)
            p_copies(1)
            for t in range(NT):
                r = rows_of(t)
                ps, sg = filled(act, ("Y", t))
                copy(YT[:, 0:3, cols_of(t)],
                     ps[:, 0:3 * P].rearrange("p (k n) -> p k n", k=3)[:, :, 0:r], sg)
            columns_hi(10)
            c_copies(2)

            def mixed_hi(t):
                emptied(act, ("P", 0, t // 3))
                emptied(act, ("P", 1, t // 3))
                emptied(act, ("Y", t))
                for j in range(3):
                    for c in {t // 3, min(2, (P * t + rows_of(t) - 1 - CHUNKS[1][0]) // CHUNKS[1][1] + 1)} \
                            if t >= 3 else {0}:
                        emptied(act, ("B", j, c))
                if t == 0:
                    for c in range(3):
                        filled(act, ("B", 2, c))
                tokens_hi(0, t, B_f)

            mixed_hi(0)
            for k in range(KD):
                act.wait_ge(s_wo[0 if k < 4 else 1 if k < 7 else 2], (64, 48, 16)[0 if k < 4 else 1 if k < 7 else 2])
                hi_of(act, ("O", k))
            mixed_hi(1)
            mixed_hi(2)
            ps, sg = filled(act, ("TB",))
            copy(outb, ps[0:18, 0:DB], sg)
            ps, sg = filled(act, ("TP",))
            copy(outp, ps[0:79, 0:DC], sg)
            for t in range(NT + 1):
                if t + 3 < NT:
                    mixed_hi(t + 3)
                if t < NT:
                    emptied(act, ("O1", t, 0))
                    emptied(act, ("O1", t, 1))
                    if t >= 2:
                        filled(act, ("T", 2, t - 2, 1))
                    norm_act(2, t, X[:, t, :])
                if t > 0:
                    emptied(act, ("T", 2, t - 1, 0))
                    emptied(act, ("T", 2, t - 1, 1))
                    tokens_hi(2, t - 1, B_f)

            def queries_ready(f):
                act.wait_ge(s_ws[f % 3], 16 * ((4, 4, 3)[f % 3] + f // 3 + 1))

            for q in range(2):
                queries_ready(q)
                hi_of(act, ("Q", q))
            for q in range(4):
                ps, sg = filled(act, ("TK", q))
                copy(KT[:, 2 * q:2 * q + 2, :], ps[:, :].rearrange("p (k n) -> p k n", k=2), sg)
            def exps(n):
                ps, sg = filled(act, ("S", n))
                act.wait_ge(s_mx, n + 1)
                if n >= 2:
                    filled(act, ("PT", n - 2))
                for a in range(2):
                    ins = nc.scalar.activation(PR[n % 2][:, a, :], ps[:, MEM * a:MEM * a + MEM], ACT.Exp,
                                               bias=stat[:, 260 + 2 * (n % 2) + a:261 + 2 * (n % 2) + a],
                                               scale=XD ** -0.5,
                                               accum_out=stat[:, 264 + 2 * (n % 2) + a:265 + 2 * (n % 2) + a])
                ins.then_inc(sg, 1)

            act.wait_ge(s_kout, 32)
            for f in range(KD):
                if f + 2 < KD:
                    queries_ready(f + 2)
                    hi_of(act, ("Q", f + 2))
                for c, (c0, cn) in enumerate(CHUNKS):
                    ps, sg = filled(act, ("Q", f, c))
                    copy(QT[:, f, c0:c0 + cn], ps[:, 0:cn], sg)
                if f == KD - 2:
                    exps(0)

            def value_hi(h):
                for e in range(2):
                    for c in range(2):
                        ps, _ = filled(act, ("PV", h, e, c))
                        nc.scalar.activation(A_hi[:, 2 * h + e, 512 * c:512 * c + 512], ps[:, :],
                                             ACT.Copy).then_inc(s_oh, 1)

            for n in range(16):
                if n > 0:
                    exps(n)
                if n in (5, 9, 13):
                    value_hi(n // 4 - 1)
                if n == 5:
                    for h in range(XH):
                        ps, sg = filled(act, ("SS", h))
                        act.wait_ge(s_mxs, XH)
                        nc.scalar.activation(PS[:, h, :], ps[0:TS, 0:MEM], ACT.Exp,
                                             bias=stat[0:TS, 268 + h:269 + h], scale=XD ** -0.5,
                                             accum_out=stat[0:TS, 272 + h:273 + h]).then_inc(sg, 1)
            value_hi(3)
            act.wait_ge(s_wx, 32)
            for k in range(KD):
                hi_of(act, ("XA", k))
            ps, sg = filled(act, ("TO",))
            nc.scalar.activation(A_hi[:, :, SEQ:N], ps[:, :].rearrange("p (k n) -> p k n", k=KD),
                                 ACT.Copy).then_inc(s_oh, 1)
            act.wait_ge(s_wx, 48)
            for k in range(KD):
                hi_of(act, ("XB", k))
            for t in range(NT + 2):
                if t < NT:
                    emptied(act, ("O2", t, 1))
                    if t >= 2:
                        filled(act, ("T", 3, t - 2, 1))
                        act.wait_ge(s_xnd[t % 2], 16 * (t // 2))
                    norm_act(3, t, X[:, t, :])
                    act.wait_ge(s_dg, NT + t + 1)
                    r = rows_of(t)
                    nc.scalar.activation(xn2[0:r, t % 2], X[0:r, t, :], ACT.Copy,
                                         scale=stat[0:r, 140 + t:141 + t]).then_inc(s_xn[3], 1)
                if t >= 2:
                    r = rows_of(t - 2)
                    ps, sg = filled(act, ("R", t - 2))
                    if t >= 4:
                        filled(act, ("L", t - 4))
                    copy(rts[t % 2][:, 0:r], ps[0:LG, 0:r], sg)
            act.wait_ge(s_gd, 1)
            nc.scalar.activation(gate[:, 0:9], gate[:, 0:9], ACT.Exp)
            nc.scalar.activation(gate[:, 9:45], gate[:, 9:45], ACT.Exp).then_inc(s_ge, 1)

            def sil(s, b, signal):
                nc.scalar.activation(SIL[s], bank[b][:, 0:FE], ACT.Silu).then_inc(signal, 1)

            def ht(s, signal):
                copy(HT[s], bank[B_TH][:, 0:2 * P].rearrange("p (k n) -> p k n", k=2), signal)

            def y0(s, signal):
                copy(YO[s][:, 0:512], bank[B_Y[0]][:, :], signal)

            act.wait_ge(m_ab[0], 1)
            sil(0, B_AB[0], m_sil[0])
            with act.Fori(0, NE // 2 - 1) as i:
                for e0, s in ((1, 1), (2, 0)):
                    q = 1 - s
                    n = i + 1 if s else i + 2
                    act.wait_ge(m_ab[s], n)
                    sil(s, B_AB[s], m_sil[s])
                    act.wait_ge(m_th[q], i + 1)
                    ht(q, m_ht[q])
                    act.wait_ge(m_y[q], i + 1)
                    act.wait_ge(m_sc[q], 16 * i + 16)
                    y0(q, m_yo0[q])
            NH = NE // 2
            act.wait_ge(m_ab[1], NH)
            sil(1, B_AB[1], m_sil[1])
            for q in range(2):
                act.wait_ge(m_th[q], NH)
                ht(q, m_ht[q])
                act.wait_ge(m_y[q], NH)
                act.wait_ge(m_sc[q], 16 * NH)
                y0(q, m_yo0[q])
            act.wait_ge(o_go, 1)
            n_spill = act.value_load(spx[0:1, 16:17], min_val=0, max_val=SPILL)
            with act.If(n_spill > 0):
                with act.Fori(0, SPILL) as q:
                    act.wait_ge(o_ab, q + 1)
                    sil(0, B_AB[0], o_sil)
                    act.wait_ge(o_th, q + 1)
                    ht(0, o_ht)
                    act.wait_ge(o_y, q + 2)
                    act.wait_ge(o_sc, 16 * q + 16)
                    y0(0, o_yo)
            for t in range(NT):
                act.wait_ge(s_fadd, t + 1)
                norm_act(0, t, X[:, t, :])

        @block.vector
        def _(dve):
            chain = [0]

            def link(ins):
                chain[0] += 1
                ins.then_inc(s_dv, 1)
                dve.wait_ge(s_dv, chain[0])

            tt, ts_, stt = nc.vector.tensor_tensor, nc.vector.tensor_scalar, nc.vector.scalar_tensor_tensor

            def inv_root(a, root, r0, tmp, out):
                link(nc.vector.reciprocal(r0, root))
                link(stt(tmp, r0, -0.5, a, ALU.mult, ALU.mult))
                link(tt(tmp, tmp, r0, ALU.mult))
                link(stt(out, tmp, 1.5, r0, ALU.add, ALU.mult))

            def col(c, r):
                return stat[0:r, c:c + 1]

            def rstd(s, t):
                r = rows_of(t)
                c = 40 * s + t
                dve.wait_ge(s_rt[s], t + 1)
                link(ts_(col(280, r), col(c, r), 1.0 / D, EPS, ALU.mult, ALU.add))
                inv_root(col(280, r), col(c + 10, r), col(281, r), col(282, r), col(c + 20, r))
                return col(c + 20, r)

            def norm_dve(s, t, src):
                r = rows_of(t)
                g = rstd(s, t)
                ts_(xn2[0:r, t % 2], src[0:r], g, None, ALU.mult).then_inc(s_xn[s], 1)

            def norm_out(s, t, dst, vec):
                r = rows_of(t)
                for q in range(2):
                    ps, sg = filled(dve, ("T", s, t, q))
                    tt(dst[:, 4 * q:4 * q + 4, 0:r],
                       ps[:, :].rearrange("p (k n) -> p k n", k=4)[:, :, 0:r],
                       pv[:, vec + 4 * q:vec + 4 * q + 4].unsqueeze(2).broadcast_to([P, 4, r]),
                       ALU.mult).then_inc(sg, 1)

            def tokens_lo(stage, t, src, dst):
                dve.wait_ge(x_hi[stage], t + 1)
                tt(dst[:, :, cols_of(t)], src[:, :, cols_of(t)], A_hi[:, :, cols_of(t)].bitcast(F32),
                   ALU.subtract).then_inc(x_lo[stage], 1)

            def diagonal_1(t):
                r = rows_of(t)
                g = rstd(1, t)
                if t >= 2:
                    filled(dve, ("N1", t - 2))
                ts_(diag[0:r, t % 2, 0:r], ident[0:r, 0:r], g, None, ALU.mult).then_inc(s_dg, 1)

            def scaled(t):
                r = rows_of(t)
                dve.wait_ge(s_xg, t + 1)
                ps, sg = filled(dve, ("N1", t))
                link(tt(Y_f[:, :, cols_of(t)], Y_f[:, :, cols_of(t)],
                        ps[:, 0:r].unsqueeze(1).broadcast_to([P, KD, r]), ALU.mult))
                nc.vector.sem_inc(s_xs, 1)
                nc.vector.sem_inc(sg, 1)

            dve.wait_ge(s_cst, 32)
            diagonal_1(0)
            lo_of(nc.vector, "v", ("U", 0))
            lo_of(nc.vector, "v", ("U", 1))
            scaled(0)
            tokens_lo(1, 0, Y_f, Y_lo)
            lo_of(nc.vector, "v", ("U", 2))
            lo_of(nc.vector, "v", ("U", 3))
            diagonal_1(1)
            for k in range(4, KD):
                lo_of(nc.vector, "v", ("U", k))
            for t in range(1, NT):
                if t + 1 < NT:
                    diagonal_1(t + 1)
                scaled(t)
                if t >= 4:
                    for k in range(2 * (t - 4), min(2 * (t - 3), KD)):
                        lo_of(nc.vector, "v", ("V", k))
                tokens_lo(1, t, Y_f, Y_lo)

            dve.wait_ge(s_rv, 48)
            dve.wait_ge(s_zero, 2)
            for t in range(NT):
                r = rows_of(t)
                emptied(dve, ("V", t))
                if t > 0:
                    dve.wait_ge(s_bn, t)
                link(nc.vector.bn_stats(bst[0:r, 36:42], V[0:r, t, :]))
                nc.vector.bn_aggr(bst[0:r, 42 + 2 * t:44 + 2 * t], bst[0:r, 36:42]).then_inc(s_bn, 1)
            dve.wait_ge(s_bn, NT)
            mv = bst[:, 42:60].rearrange("p (t c) -> p t c", c=2)
            ts_(bst[:, 18:27], mv[:, :, 1], EPS, None, ALU.add).then_inc(s_bn, 1)
            dve.wait_ge(s_bn, NT + 1)
            ps, sg = filled(dve, ("WS",))
            tt(v3(wst, 0, AH, P), ps[:, :].rearrange("p (h i) -> p h i", h=AH),
               mask.unsqueeze(1).broadcast_to([P, AH, P]), ALU.mult).then_inc(sg, 1)
            ps, sg = filled(dve, ("W8",))
            tt(wst8[0:TS, :].rearrange("p (h i) -> p h i", h=AH),
               ps[0:TS, 0:AH * TS].rearrange("p (h i) -> p h i", h=AH),
               mask[0:TS, 0:TS].unsqueeze(1).broadcast_to([TS, AH, TS]), ALU.mult).then_inc(sg, 1)
            ps, sg = filled(dve, ("SC",))
            nc.vector.tensor_copy(sct, ps[:, 0:48].rearrange("p (j n) -> p j n", j=3)).then_inc(sg, 1)
            ps, sg = filled(dve, ("SP",))
            nc.vector.tensor_copy(spt, ps[:, 0:240].rearrange("p (j n) -> p j n", j=2)).then_inc(sg, 1)

            dve.wait_ge(s_lrt, 1)
            inv_root(bst[:, 18:27], bst[:, 27:36], bst[:, 0:9], bst[:, 9:18], stat[:, 290:299])
            for t in range(NT):
                r = rows_of(t)
                v = V[0:r, t, :]
                link(ts_(v, v, bst[0:r, 42 + 2 * t:43 + 2 * t], stat[0:r, 290 + t:291 + t],
                         ALU.subtract, ALU.mult))
                link(tt(v, v, rv[0:r, R_LNG:R_LNG + DA], ALU.mult))
                tt(v, v, rv[0:r, R_LNB:R_LNB + DA], ALU.add).then_inc(s_vln, 1)

            def conv_tile(j):
                w = [pv[:, V_CONV + 3 * j + k:V_CONV + 3 * j + k + 1] for k in range(3)]
                link(nc.vector.tensor_copy(zcs[:, :, 0:2], sct[:, j, :].rearrange("p (b r) -> p b r", b=NB)))
                for c, (c0, cn) in enumerate(CHUNKS):
                    emptied(dve, ("C", j, c))
                    ps, sg = filled(dve, ("X", j, c))
                    n = min(cn, SEQ - c0)
                    z = zc[:, 2 + c0:2 + c0 + n]
                    ins = tt(z, ps[:, 0:n], z, ALU.mult)
                    if c == 2:
                        ins = tt(zcs[:, :, 2:], ps[:, n:cn].rearrange("p (b l) -> p b l", b=NB),
                                 zcs[:, :, 2:], ALU.mult)
                    ins.then_inc(sg, 1)
                for c in range(3):
                    emptied(dve, ("X", j, c))
                cp = YT[:, 3 + j, 0:SEQ]
                cs = YT[:, 3 + j, SEQ:N].rearrange("p (b l) -> p b l", b=NB)
                ts_(cp, zc[:, 0:SEQ], w[0], None, ALU.mult)
                link(ts_(cs, zcs[:, :, 0:DS], w[0], None, ALU.mult))
                for k in (1, 2):
                    stt(cp, zc[:, k:k + SEQ], w[k], cp, ALU.mult, ALU.add)
                    link(stt(cs, zcs[:, :, k:k + DS], w[k], cs, ALU.mult, ALU.add))
                nc.vector.tensor_copy(tailb[:, j, 0:16].rearrange("p (b r) -> p b r", b=NB), zcs[:, :, DS:DS + 2])
                nc.vector.tensor_copy(tailb[:, j, 16:18], zc[:, SEQ:SEQ + 2]).then_inc(s_tail, 1)
                for c, (c0, cn) in enumerate(CHUNKS):
                    ps, sg = filled(dve, ("B", j, c))
                    y = YT[:, 3 + j, c0:c0 + cn]
                    tt(y, ps[:, 0:cn], y, ALU.mult).then_inc(sg, 1)

            def gate_mul(g, h):
                t0, n = (4 * g, 4) if g < 2 else (NPT, 1)
                r = rows_of(t0)
                bs = (V_BS if g < 2 else V_BS8) + h
                dve.wait_ge(s_ug, t0 + n)
                ps, sg = filled(dve, ("G", g, h))
                u = U[0:r, t0:t0 + n, AHD * h:AHD * h + AHD]
                stt(u, ps[0:r, 0:n * AHD].rearrange("p (t d) -> p t d", t=n), pv[0:r, bs:bs + 1], u,
                    ALU.add, ALU.mult).then_inc(sg, 1)

            def pooling(j):
                pzs, pas, pbs = (x[:, LP:LZ].rearrange("p (b l) -> p b l", b=NB) for x in (pz, pa, pb))
                if j == 0:
                    emptied(dve, ("SP",))
                else:
                    filled(dve, ("P", 0, 2))
                nc.vector.memset(pz[:, 0:POOLB], 0.0)
                link(nc.vector.tensor_copy(pzs[:, :, 0:POOLB],
                                           spt[:, j, :].rearrange("p (b l) -> p b l", b=NB)))
                for c in range(3):
                    emptied(dve, ("Z", j, c))
                src, d = (pz, pzs), 1
                bufs = [(pa, pas), (pb, pbs)]
                levels = 2 if j == 0 else 4
                lo = None
                for lv in range(levels):
                    p = slice(64 if lv == levels - 1 else 0, P)
                    dst = bufs[lv % 2]
                    a = 2 * d - 1
                    tt(dst[0][p, a:LP], src[0][p, a:LP], src[0][p, a - d:LP - d], ALU.add)
                    link(tt(dst[1][p, :, a:], src[1][p, :, a:], src[1][p, :, a - d:LS - d], ALU.add))
                    if lv == levels - 2:
                        lo = dst
                    src, d = dst, 2 * d
                for p0, s, w in ((0, lo, POOL_W[2 * j]), (64, src, POOL_W[2 * j + 1])):
                    p = slice(p0, p0 + 64)
                    stt(pd[p, 16:SEQ], s[0][p, POOLB + 16:LP], 1.0 / w, pz[p, POOLB + 16:LP],
                        ALU.mult, ALU.subtract)
                    stt(pd[p, SEQ:N].rearrange("p (b l) -> p b l", b=NB), s[1][p, :, POOLB:], 1.0 / w,
                        pzs[p, :, POOLB:], ALU.mult, ALU.subtract)
                    link(tt(ptmp[p, :], s[0][p, POOLB:POOLB + 16], invt[p, j, :], ALU.mult))
                tt(pd[:, 0:16], ptmp[:, :], pz[:, POOLB:POOLB + 16], ALU.subtract)
                nc.vector.tensor_copy(tailp[:, j, 0:TS].rearrange("p (b l) -> p b l", b=NB), pzs[:, :, POOLB:])
                nc.vector.tensor_copy(tailp[:, j, TS:TS + POOLB], pz[:, LP - POOLB:LP]).then_inc(s_pd, 1)

            link(nc.vector.memset(zc[:, 0:2], 0.0))
            emptied(dve, ("SC",))
            pooling(0)
            conv_tile(0)
            pooling(1)
            for g in range(3):
                for h in range(AH):
                    gate_mul(g, h)
            conv_tile(1)
            conv_tile(2)

            def add_residual(name, t, h):
                r = rows_of(t)
                if name == "O1" and h == 0:
                    dve.wait_ge(s_xr[t // 3], 48)
                ps, sg = filled(dve, (name, t, h))
                x = X[0:r, t, 512 * h:512 * h + 512]
                tt(x, x, ps[0:r, :], ALU.add).then_inc(sg, 1)

            tokens_lo(0, 0, B_f, B_lo)
            for k in range(KD):
                lo_of(nc.vector, "v", ("O", k))
            tokens_lo(0, 1, B_f, B_lo)
            tokens_lo(0, 2, B_f, B_lo)
            dve.wait_ge(s_tail, 3)
            for t in range(NT + 1):
                if t < NT:
                    for h in range(2):
                        add_residual("O1", t, h)
                    norm_dve(2, t, X[:, t, :])
                if t > 0:
                    norm_out(2, t - 1, B_f[:, :, cols_of(t - 1)], V_GX)
                if t + 3 < NT:
                    tokens_lo(0, t + 3, B_f, B_lo)
                if t > 0:
                    tokens_lo(2, t - 1, B_f, B_lo)
            for name, dst in (("K", Kn), ("V", VP)):
                for m in range(MT):
                    for h in range(2):
                        ps, sg = filled(dve, (name, m, h))
                        nc.vector.tensor_copy(dst[:, m, 512 * h:512 * h + 512], ps[:, :]).then_inc(sg, 1)

            def neg_max(n):
                ps, _ = filled(dve, ("S", n))
                c = 260 + 2 * (n % 2)
                link(nc.vector.tensor_reduce(stat[:, 276:278], ps[:, :].rearrange("p (a m) -> p a m", a=2),
                                             axis=AX.X, op=ALU.max, negate=True))
                ts_(stat[:, c:c + 2], stat[:, 276:278], XD ** -0.5, None, ALU.mult).then_inc(s_mx, 1)
                dve.wait_ge(s_mx, n + 1)

            def normalise(n):
                emptied(dve, ("S", n))
                c = 264 + 2 * (n % 2)
                link(nc.vector.reciprocal(stat[:, 278:280], stat[:, c:c + 2]))
                for a in range(2):
                    p_ = PR[n % 2][:, a, :]
                    ins = ts_(p_, p_, stat[:, 278 + a:279 + a], None, ALU.mult)
                ins.then_inc(s_pn, 1)
                dve.wait_ge(s_pn, n + 1)

            def turned(n):
                h, tp = n // 4, n % 4
                ps, sg = filled(dve, ("PT", n))
                nc.vector.tensor_copy(PT[h % 2][:, :, MEM * tp:MEM * tp + MEM],
                                      ps[:, :].rearrange("p (m n) -> p m n", m=MT)).then_inc(sg, 1)

            def own_columns(tile, src):
                n = NB - 1
                nc.vector.tensor_copy(
                    tile[:, 0:(TS + DS) * n].rearrange("p (b l) -> p b l", b=n)[:, :, 0:DS],
                    src[:, 0:DS * n].rearrange("p (b l) -> p b l", b=n))
                return nc.vector.tensor_copy(tile[:, (TS + DS) * n:(TS + DS) * n + DS], src[:, DS * n:TS])

            def value_lo(h, parts=(0, 1, 2, 3)):
                for part in parts:
                    e, c = part // 2, part % 2
                    ps, sg = filled(dve, ("PV", h, e, c))
                    dve.wait_ge(s_oh, 4 * h + part + 1)
                    cols = slice(512 * c, 512 * c + 512)
                    link(tt(B_lo[:, 2 * h + e, cols], ps[:, :], A_hi[:, 2 * h + e, cols].bitcast(F32),
                            ALU.subtract))
                    nc.vector.sem_inc(sg, 1)
                    nc.vector.sem_inc(x_lo[3], 1)

            neg_max(0)
            neg_max(1)
            normalise(0)
            dve.wait_ge(s_qz, 1)
            for c in range(3):
                emptied(dve, ("Q", KD - 1, c))
            for f in range(KD):
                own_columns(QM[f], QT[:, f, SEQ:N]).then_inc(s_qm, 1)
            for n in range(16):
                if n + 2 < 16:
                    neg_max(n + 2)
                if n + 1 < 16:
                    normalise(n + 1)
                if n == 4:
                    value_lo(0)
                turned(n)
                if n > 8 and n % 4:
                    value_lo(n // 4 - 1, ((0,), (1,), (2, 3))[n % 4 - 1])
                if n == 4:
                    for h in range(XH):
                        ps, _ = filled(dve, ("SS", h))
                        link(nc.vector.tensor_reduce(stat[0:TS, 276:277], ps[0:TS, 0:MEM], axis=AX.X, op=ALU.max,
                                                     negate=True))
                        ts_(stat[0:TS, 268 + h:269 + h], stat[0:TS, 276:277], XD ** -0.5, None, ALU.mult) \
                            .then_inc(s_mxs, 1)
                        dve.wait_ge(s_mxs, h + 1)
                if n == 6:
                    for h in range(XH):
                        emptied(dve, ("SS", h))
                    link(nc.vector.reciprocal(stat[0:TS, 283:287], stat[0:TS, 272:276]))
                    for h in range(XH):
                        ins = ts_(PS[:, h, :], PS[:, h, :], stat[0:TS, 283 + h:284 + h], None, ALU.mult)
                    ins.then_inc(s_pns, 1)
            dve.wait_ge(s_qz, 2)
            ps, sg = filled(dve, ("PTS",))
            for g in range(XH * MT):
                ins = own_columns(PTM[:, 512 * g:512 * g + 512], ps[:, TS * g:TS * g + TS])
            ins.then_inc(sg, 1)
            value_lo(3)
            for k in range(KD):
                lo_of(nc.vector, "v", ("XA", k))
            for h in range(XH):
                ps, sg = filled(dve, ("PVS", h))
                nc.vector.tensor_copy(ON[:, XD * h:XD * h + XD], ps[0:TS, 0:XD]).then_inc(sg, 1)
            add_residual("O2", 0, 0)
            ps, sg = filled(dve, ("TO",))
            dve.wait_ge(s_oh, 17)
            link(tt(B_lo[:, :, SEQ:N], ps[:, :].rearrange("p (k n) -> p k n", k=KD),
                    A_hi[:, :, SEQ:N].bitcast(F32), ALU.subtract))
            nc.vector.sem_inc(sg, 1)
            nc.vector.sem_inc(x_lo[3], 1)
            for t in range(1, NT):
                add_residual("O2", t, 0)

            def add_bias(t):
                r = rows_of(t)
                ps, sg = filled(dve, ("L", t))
                tt(lgm[0:r, LG * t:LG * t + LG], ps[0:r, 0:LG], rv[0:r, R_BIAS:R_BIAS + LG], ALU.add).then_inc(sg, 1)

            def route(b_):
                tiles = range(GT * b_, GT * b_ + GT)
                for t in tiles:
                    emptied(dve, ("L", t))
                lg = lgm[:, LG * GT * b_:LG * GT * (b_ + 1)].rearrange("p (t c) -> p t c", t=GT)
                u = ui[:, :].rearrange("p (t c) -> p t c", t=GT)
                for j, t in enumerate(tiles):
                    ins = nc.vector.max(top[:, 16 * t:16 * t + 8], lg[:, j, 0:8])
                link(ins)
                for j, t in enumerate(tiles):
                    ins = nc.vector.max_index(u[:, j, 0:8], top[:, 16 * t:16 * t + 8], lg[:, j, 0:8])
                link(ins)
                link(nc.vector.tensor_copy(gix, u[:, :, 0]))
                link(tt(gone, iota[:, 0:NG].unsqueeze(1).broadcast_to([P, GT, NG]),
                        gix.unsqueeze(2).broadcast_to([P, GT, NG]), ALU.is_equal))
                for j in range(GT):
                    ins = tt(own[:, j, :].rearrange("p (g e) -> p g e", g=NG),
                             lg[:, j, 8:8 + NE].rearrange("p (g e) -> p g e", g=NG),
                             gone[:, j, :].unsqueeze(2).broadcast_to([P, NG, EPG]), ALU.mult)
                link(ins)
                for j in range(GT):
                    ins = nc.vector.tensor_reduce(esel[:, j, :], own[:, j, :].rearrange("p (g e) -> p e g", g=NG),
                                                  axis=AX.X, op=ALU.add)
                link(ins)
                for j, t in enumerate(tiles):
                    ins = nc.vector.max(top[:, 16 * t + 8:16 * t + 16], esel[:, j, :])
                link(ins)
                for j, t in enumerate(tiles):
                    ins = nc.vector.max_index(u[:, j, 8:16], top[:, 16 * t + 8:16 * t + 16], esel[:, j, :])
                link(ins)
                ex = EX[:, GT * b_:GT * b_ + GT, :]
                link(nc.vector.tensor_copy(ex, u[:, :, 8:10]))
                link(stt(ex, gix.unsqueeze(2).broadcast_to([P, GT, 2]), float(EPG), ex, ALU.mult, ALU.add))
                both = RM12[:, 2 * GT * b_:2 * GT * (b_ + 1), :]
                link(tt(both, iota.unsqueeze(1).broadcast_to([P, 2 * GT, NE]),
                        ex.rearrange("p t k -> p (t k)").unsqueeze(2).broadcast_to([P, 2 * GT, NE]), ALU.is_equal))
                if tiles[-1] == NT - 1:
                    link(nc.vector.memset(RM12[TS:P, 2 * NT - 2:2 * NT, :], 0.0))
                pair = both.rearrange("p (t k) e -> p t k e", k=2)
                link(tt(RM[:, GT * b_:GT * b_ + GT, :], pair[:, :, 0, :], pair[:, :, 1, :], ALU.add))
                for t in tiles:
                    tt(RMA[:, t + 1, :], RMA[:, t, :], RM[:, t, :], ALU.add).then_inc(s_rma, 1)
                    dve.wait_ge(s_rma, t + 1)

            def place(b_):
                ps, sg = filled(dve, ("RK", b_))
                for j in range(GT):
                    t = GT * b_ + j
                    ins = tt(rank_of[:, 2 * j:2 * j + 2, :], RM12[:, 2 * t:2 * t + 2, :],
                             ps[:, NE * j:NE * j + NE].unsqueeze(1).broadcast_to([P, 2, NE]), ALU.mult)
                ins.then_inc(sg, 1)
                emptied(dve, ("RK", b_))
                ex = EX[:, GT * b_:GT * b_ + GT, :].rearrange("p t k -> p (t k)")
                link(nc.vector.tensor_reduce(rk, rank_of, axis=AX.X, op=ALU.add))
                link(nc.vector.tensor_copy(ri.bitcast(I32), rk))
                link(ts_(ri.bitcast(I32), ri.bitcast(I32), 7, None, ALU.arith_shift_right))
                link(nc.vector.tensor_copy(rq, ri.bitcast(I32)))
                stt(ra, rq, -float(P), rk, ALU.mult, ALU.add)
                stt(rb, ex, float(NPT - 1), rq, ALU.mult, ALU.add)
                link(ts_(rc, rq, 1.0, None, ALU.is_ge))
                stt(ra, ra, float(NPLACE), ex, ALU.mult, ALU.add)
                link(stt(rb, rb, float(NE - 1), rc, ALU.add, ALU.mult))
                link(tt(ra, ra, rb, ALU.add))
                nc.vector.tensor_copy(plc[:, 2 * GT * b_:2 * GT * (b_ + 1)], ra).then_inc(s_plc, 1)
                dve.wait_ge(s_plc, b_ + 1)

            for t in range(NT + 5):
                if t >= 7 and t % GT == 1:
                    place((t - 7) // GT)
                if t < NT:
                    add_residual("O2", t, 1)
                    rstd(3, t)
                    nc.vector.sem_inc(s_dg, 1)
                if t == 0:
                    link(nc.vector.memset(regS[:, 0:1184 + 2 * NT], 0.0))
                if 0 <= t - 1 < NT:
                    if t >= 4:
                        filled(dve, ("R", t - 4))
                    norm_out(3, t - 1, YT3[(t - 1) % 3], V_GFFN)
                if 0 <= t - 3 < NT:
                    add_bias(t - 3)
                    if t % GT == 2:
                        route(t // GT - 1)

            ps, sg = filled(dve, ("CN",))
            ts_(cni[:, :], ps[:, 0:NE], -1.0, None, ALU.add).then_inc(sg, 1)
            emptied(dve, ("CN",))
            link(ts_(cni[:, :], cni[:, :], 7, None, ALU.arith_shift_right))
            over = re_[:, 0, :]
            link(ts_(over, cni[:, :], 0.0, None, ALU.max))
            src, k = over, 1
            while k < NE:
                dst = re_[:, 1 if src is not None and k in (1, 4, 16) else 2, :]
                nc.vector.tensor_copy(dst[:, 0:k], src[:, 0:k])
                link(tt(dst[:, k:], src[:, k:], src[:, 0:NE - k], ALU.add))
                src, k = dst, 2 * k
            ends = src
            q3 = rq16.rearrange("p (q e) -> p q e", q=16)
            link(tt(q3, ends[0:1].unsqueeze(1).broadcast_to([1, 16, NE]),
                    iota[0:1, 0:16].unsqueeze(2).broadcast_to([1, 16, NE]), ALU.is_le))
            link(nc.vector.tensor_reduce(rs[0:1, 0:16], q3, axis=AX.X, op=ALU.add))
            link(ts_(spx[0:1, 0:16], rs[0:1, 0:16], float(NE - 1), None, ALU.min))
            link(nc.vector.tensor_copy(spx[0:1, 16:17], ends[0:1, NE - 1:NE]))
            link(tt(q3, q3, over[0:1].unsqueeze(1).broadcast_to([1, 16, NE]), ALU.mult))
            link(nc.vector.tensor_reduce(rs[0:1, 16:32], q3, axis=AX.X, op=ALU.add))
            link(tt(rs[0:1, 16:32], iota[0:1, 0:16], rs[0:1, 16:32], ALU.subtract))
            link(ts_(rs[0:1, 0:16], rs[0:1, 0:16], float(NE - 1), None, ALU.min))
            link(stt(rs[0:1, 16:32], rs[0:1, 0:16], float(NPT), rs[0:1, 16:32], ALU.mult, ALU.add))
            link(ts_(spx[0:1, 32:48], rs[0:1, 16:32], float(NE), float(NPLACE - 1), ALU.add, ALU.min))
            tp = top[:, :].rearrange("p (t c) -> p t c", c=16)
            lg3 = lgm[:, :].rearrange("p (t c) -> p t c", c=LG)
            tt(gate[:, 0:NT], tp[:, :, 9], tp[:, :, 8], ALU.subtract)
            tt(gate[:, NT:5 * NT].rearrange("p (t g) -> p t g", g=NG), lg3[:, :, 0:NG],
               tp[:, :, 0:1].broadcast_to([P, NT, NG]), ALU.subtract).then_inc(s_gd, 1)
            dve.wait_ge(s_ge, 1)
            dif, gs, w1, w2 = gate[:, 0:NT], gate[:, 5 * NT:6 * NT], gate[:, 6 * NT:7 * NT], gate[:, 7 * NT:8 * NT]
            link(nc.vector.tensor_reduce(gs, gate[:, NT:5 * NT].rearrange("p (t g) -> p t g", g=NG),
                                         axis=AX.X, op=ALU.add))
            link(stt(w1, dif, 1.0, gs, ALU.add, ALU.mult))
            link(nc.vector.reciprocal(w1, w1))
            link(tt(w2, w1, dif, ALU.mult))

            def xt(s, signal):
                for q in range(2):
                    ins = tt(XGT[s][:, 4 * q:4 * q + 4, :],
                             bank[B_TX[q]][:, :].rearrange("p (k n) -> p k n", k=4),
                             pv[:, V_GFFN + 4 * q:V_GFFN + 4 * q + 4].unsqueeze(2).broadcast_to([P, 4, P]),
                             ALU.mult)
                ins.then_inc(signal, 1)

            def hid(s, b, signal):
                tt(HID[s], SIL[s], bank[b][:, FE:2 * FE], ALU.mult).then_inc(signal, 1)

            def y1(s, signal):
                nc.vector.tensor_copy(YO[s][:, 512:1024], bank[B_Y[1]][:, :]).then_inc(signal, 1)

            NH = NE // 2
            dve.wait_ge(m_tx[0], 1)
            xt(0, m_xt[0])
            dve.wait_ge(m_sil[0], 1)
            hid(0, B_AB[0], m_hid[0])
            dve.wait_ge(m_tx[1], 1)
            xt(1, m_xt[1])
            with dve.Fori(0, NH - 1) as i:
                for e0, s in ((1, 1), (2, 0)):
                    q = 1 - s
                    n = i + 1 if s else i + 2
                    dve.wait_ge(m_sil[s], n)
                    hid(s, B_AB[s], m_hid[s])
                    dve.wait_ge(m_tx[q], i + 2)
                    xt(q, m_xt[q])
                    dve.wait_ge(m_y[q], i + 1)
                    dve.wait_ge(m_sc[q], 16 * i + 16)
                    y1(q, m_yo1[q])
            dve.wait_ge(m_sil[1], NH)
            hid(1, B_AB[1], m_hid[1])
            for q in range(2):
                dve.wait_ge(m_y[q], NH)
                dve.wait_ge(m_sc[q], 16 * NH)
                y1(q, m_yo1[q])
            dve.wait_ge(o_go, 1)
            n_spill = dve.value_load(spx[0:1, 16:17], min_val=0, max_val=SPILL)
            with dve.If(n_spill > 0):
                with dve.Fori(0, SPILL) as q:
                    dve.wait_ge(o_tx, q + 2)
                    xt(0, o_xt)
                    dve.wait_ge(o_sil, q + 1)
                    hid(0, B_AB[0], o_hid)
                    dve.wait_ge(o_y, q + 2)
                    y1(0, o_yo)

            def combine(t):
                r = rows_of(t)
                dve.wait_ge(s_xr[t % 3], 48 + 32 * (t // 3 + 1))
                x = X[0:r, t, :]
                link(stt(x, Y12[t % 3][0:r, 0, :], w1[0:r, t:t + 1], x, ALU.mult, ALU.add))
                stt(x, Y12[t % 3][0:r, 1, :], w2[0:r, t:t + 1], x, ALU.mult, ALU.add).then_inc(s_fadd, 1)

            def finish(t):
                r = rows_of(t)
                g = rstd(0, t)
                dve.wait_ge(s_fadd, t + 1)
                if t >= 2:
                    dve.wait_ge(s_fst[t % 2], 16 * (t // 2))
                stt(FO[t % 2][0:r, :], X[0:r, t, :], g, gfin[0:r, :], ALU.mult, ALU.mult).then_inc(s_fo, 1)

            dve.wait_ge(s_gf, 16)
            for t in range(NT + 1):
                if t < NT:
                    combine(t)
                if t > 0:
                    finish(t - 1)

        @block.gpsimd
        def _(g):
            def store(dst, src, signal):
                g.dma_start(dst, src).then_inc(signal, 16)

            g.memset(small[:, :], EPS).then_inc(s_zero, 1)
            g.wait_ge(s_cst, 32)
            for t in range(NT):
                r = rows_of(t)
                g.wait_ge(s_x[t % 3], 32 * (t // 3 + 1))
                x = Y_f[:, :, cols_of(t)]
                g.tensor_tensor(x, x, pv[:, V_GMIX:V_GMIX + KD].unsqueeze(2).broadcast_to([P, KD, r]),
                                ALU.mult).then_inc(s_xg, 1)
            g.memset(bst[:, :], 1.0)
            g.memset(lgm[:, :], 0.0)
            g.memset(top[:, :], 0.0)
            g.memset(idx[:, :], NOWHERE).then_inc(s_zero, 1)
            g.iota(pay[:, :], pattern=[[P, NT], [N, 2], [0, 2]], base=0, channel_multiplier=1).then_inc(s_zero, 1)
            g.wait_ge(s_zero, 2)
            wide = table.rearrange("(p c) k -> p (c k)", p=P)
            for c in range(0, 2 * NPLACE, 3 * NE):
                store(wide[:, c:c + 3 * NE], idx[:, :], s_pre)
            pay4 = pay[:, :].rearrange("p (t k c) -> p t k c", k=2, c=2)
            g.wait_ge(s_zero, 3)
            g.iota(pay4[:, :, :, 0], pattern=[[P, NT], [0, 2]], base=0, channel_multiplier=1).then_inc(s_zero, 1)
            store(o_["new_pool_sample"][0, :, 0:POOLB - DS, :], i_["state_pool"][0, :, DS:POOLB, :], s_outs)
            for w in range(5):
                lo_of(g, "g", ("F", w))
            g.wait_ge(s_vln, NT)
            store(o_["new_chunk_v_sample"][0].rearrange("b s d -> (b s) d"), V[0:TS, NPT, :], s_outs)
            for w in range(5, 11):
                lo_of(g, "g", ("F", w))
            emptied(g, ("TB",))
            store(o_["new_conv_sample"][0].rearrange("b r d -> (b r) d"), outb[0:16, :], s_outs)
            store(o_["new_conv_prompt"][0, 0], outb[16:18, :], s_outs)
            emptied(g, ("TP",))
            store(o_["new_pool_sample"][0, :, POOLB - DS:POOLB, :], outp[0:TS, :], s_outs)
            store(o_["new_pool_prompt"][0, 0], outp[TS:TS + POOLB, :], s_outs)
            lo_of(g, "g", ("Q", 0))
            lo_of(g, "g", ("Q", 1))
            for name, out, src in (("K", "new_mem_k_prompt", Kn), ("V", "new_mem_v_prompt", VP)):
                for m in range(MT):
                    for h in range(2):
                        emptied(g, (name, m, h))
                store(o_[out][0, 0].rearrange("(m p) h e -> p m (h e)", p=P), src, s_kout)
            for f in range(2, KD):
                lo_of(g, "g", ("Q", f))
                if f == 2:
                    filled(g, ("T", 2, NT - 1, 1))
                    for h in range(2):
                        filled(g, ("V", 1, h))
                    for q in QM:
                        ins = g.memset(q, 0.0)
                    ins.then_inc(s_qz, 1)
            filled(g, ("S", 15))
            filled(g, ("S", 14))
            g.memset(PTM, 0.0).then_inc(s_qz, 1)
            for k in range(KD):
                lo_of(g, "g", ("XB", k))
            g.wait_ge(s_zero, 4)
            g.wait_ge(s_pre, 16 * (2 * NPLACE // (3 * NE)))
            plc3 = plc[:, :].rearrange("p (t k) -> p t k", k=2)
            for s in range(2):
                store(gixs[s][:, :], table[0:P, :], m_sc[s])
            store(oix[:, :], table[0:P, :], o_sc)
            g.sem_inc(o_y, 1)
            g.sem_inc(o_tx, 1)
            g.sem_inc(o_yo, 1)
            for s in range(2):
                g.wait_ge(m_sc[s], 16)
            g.wait_ge(o_sc, 16)
            for t in range(NT):
                r = rows_of(t)
                if t == NT - GT:
                    filled(g, ("O2", NT - 1, 1))
                    g.memset(regA[:, 0:2 * D], 0.0).then_inc(s_zero, 1)
                g.wait_ge(s_plc, t // GT + 1)
                for k in range(2):
                    g.indirect_dma_start(
                        out=table, out_offset=bass.IndirectOffsetOnAxis(ap=plc3[0:r, t, k:k + 1], axis=0),
                        in_=pay4[0:r, t, k, :], in_offset=None,
                        bounds_check=P * NPLACE - 1, oob_is_err=False).then_inc(s_scat, 16)
            g.wait_ge(s_zero, 5)
            g.sem_inc(m_yo0[1], 1)
            g.sem_inc(m_yo1[1], 1)
            g.wait_ge(s_xnd[0], 16 * 5)
            g.wait_ge(s_xnd[1], 16 * 4)
            g.wait_ge(s_idx, 16)
            last_token, last_row = g.to_reg(N - 1), g.to_reg(2 * N - 1)

            def waited():
                g.sem_inc(s_waited, 1)
                g.wait_ge(s_waited, 1)

            def gather(s, ix, signal):
                g.indirect_dma_start(out=XG[s], out_offset=None, in_=xn_dram,
                                     in_offset=bass.IndirectOffsetOnAxis(ap=ix[:, 0:1], axis=0),
                                     bounds_check=last_token, oob_is_err=False).then_inc(signal, 16)

            def scatter(s, ix, signal):
                g.indirect_dma_start(out=y_dram, out_offset=bass.IndirectOffsetOnAxis(ap=ix[:, 1:2], axis=0),
                                     in_=YO[s], in_offset=None,
                                     bounds_check=last_row, oob_is_err=False).then_inc(signal, 16)

            NH = NE // 2
            for e in range(3):
                if e == 2:
                    g.wait_ge(m_tx[0], 1)
                g.tensor_copy(gixg[e % 2][:, :], idx[:, 2 * e:2 * e + 2]).then_inc(m_gi[e % 2], 1)
                g.wait_ge(m_gi[e % 2], e // 2 + 1)
                gather(e % 2, gixg[e % 2], m_g[e % 2])
            with g.Fori(0, NH - 2) as i:
                of_rows = [g.snap(4 * i + 2 * s) for s in range(2)]
                of_tokens = [g.snap(4 * i + 2 * s + 6) for s in range(2)]
                for s in range(2):
                    q = 1 - s
                    g.wait_ge(m_tx[q], i + 1 + s)
                    g.tensor_copy(gixg[q][:, :], idx[:, bass.ds(of_tokens[s], 2)]).then_inc(m_gi[q], 1)
                    g.wait_ge(m_gi[q], i + 2 + s)
                    waited()
                    gather(q, gixg[q], m_g[q])
                    g.wait_ge(m_sc[s], 16 * i + 16)
                    g.tensor_copy(gixs[s][:, :], idx[:, bass.ds(of_rows[s], 2)]).then_inc(m_si[s], 1)
                    g.wait_ge(m_si[s], i + 1)
                    g.wait_ge(m_yo0[s], i + 1 + s)
                    g.wait_ge(m_yo1[s], i + 1 + s)
                    waited()
                    scatter(s, gixs[s], m_sc[s])
            g.wait_ge(m_tx[1], NH - 1)
            g.tensor_copy(gixg[1][:, :], idx[:, 2 * NE - 2:2 * NE]).then_inc(m_gi[1], 1)
            g.wait_ge(m_gi[1], NH)
            gather(1, gixg[1], m_g[1])
            for e in range(NE - 4, NE):
                s, n = e % 2, e // 2
                g.wait_ge(m_sc[s], 16 * n + 16)
                g.tensor_copy(gixs[s][:, :], idx[:, 2 * e:2 * e + 2]).then_inc(m_si[s], 1)
                g.wait_ge(m_si[s], n + 1)
                g.wait_ge(m_yo0[s], n + 1 + s)
                g.wait_ge(m_yo1[s], n + 1 + s)
                scatter(s, gixs[s], m_sc[s])
            for s in range(2):
                g.wait_ge(m_sc[s], 16 * (NH + 1))
            g.sem_inc(o_go, 1)
            n_spill = g.value_load(spx[0:1, 16:17], min_val=0, max_val=SPILL)
            with g.If(n_spill > 0):
                with g.Fori(0, SPILL) as q:
                    g.wait_ge(o_ix, 16 * q + 16)
                    g.wait_ge(o_tx, q + 1)
                    waited()
                    gather(0, oix, o_g)
                    g.wait_ge(o_yo, 2 * q + 3)
                    waited()
                    scatter(0, oix, o_sc)
                g.wait_ge(o_sc, 16 * (SPILL + 1))
            g.sem_inc(s_moe, 1)
            for t in range(NT):
                g.wait_ge(s_fo, t + 1)
                dst = o_["y_prompt"][0, P * t:P * t + P, :] if t < NPT else \
                    o_["y_sample"].rearrange("b s d -> (b s) d")
                store(dst, FO[t % 2][0:rows_of(t), :], s_fst[t % 2])
            g.wait_ge(s_fst[0], 16 * 5)
            g.wait_ge(s_fst[1], 16 * 4)
            g.wait_ge(s_outs, 16 * 6)
            g.wait_ge(s_kout, 32)


POOL_W = (2, 4, 8, 16)
_OUTS = [("y_prompt", (1, SEQ, D)), ("y_sample", (NB, DS, D)),
         ("new_conv_prompt", (1, 1, 2, DB)), ("new_conv_sample", (1, NB, 2, DB)),
         ("new_pool_prompt", (1, 1, POOLB, DC)), ("new_pool_sample", (1, NB, POOLB, DC)),
         ("new_chunk_v_sample", (1, NB, DS, DA)),
         ("new_mem_k_prompt", (1, 1, MEM, XH, XD)), ("new_mem_v_prompt", (1, 1, MEM, XH, XD))]


def _constants():
    c = np.zeros((P, C_END), np.float32)
    i = np.arange(P)
    c[:, C_ID:C_ID + P] = i[:, None] == i[None]
    c[:, C_UP:C_UP + P] = i[:, None] < i[None]
    c[:, C_MASK:C_MASK + P] = i[:, None] <= i[None]
    c[:, C_ONE:C_ONE + P] = 1.0
    for g, w in enumerate(POOL_W):
        rows = slice(64 * (g % 2), 64 * (g % 2) + 64)
        c[rows, C_INV + 16 * (g // 2):C_INV + 16 * (g // 2) + 16] = 1.0 / np.minimum(np.arange(16) + 1, w)
    c[:, C_IOTA:C_IOTA + NE] = np.arange(NE)
    return c


def _tiles(w):
    return np.ascontiguousarray(w.reshape(-1, P, w.shape[-1]).transpose(1, 0, 2)).reshape(P, -1)


def _features(x):
    return x.reshape(-1, KD, P).transpose(2, 1, 0)


def _columns(v):
    return v.reshape(-1, P).T


def _layouts(a):
    f = np.float32
    w_in = a["w_in"][0]
    off_bb, off_bc, off_bx, off_cz = 2 * DA, 2 * DA + DB, 2 * DA + 2 * DB, 2 * DA + 3 * DB
    starts = [off_cz, off_cz + P]
    for j in range(3):
        starts += [off_bc + P * j, off_bx + P * j, off_bb + P * j]
    wp = np.zeros((P, 2 * P), f)
    for g in range(4):
        p0, j = 64 * (g % 2), g // 2
        wp[p0:p0 + 64, P * j + p0:P * j + p0 + 64] = a["w_pool"][0, g]
    w8 = np.zeros((NB, DS, AH, NB, DS), f)
    for b in range(NB):
        w8[b, :, :, b, :] = a["w_s"][0, :, :DS, :DS].transpose(1, 0, 2)
    conv = a["w_conv"][0].reshape(3, 3, P).transpose(2, 1, 0).reshape(P, 9)
    bs = a["b_s"][0].T
    bs8 = np.zeros((P, AH), f)
    bs8[:TS] = np.tile(bs[:DS], (NB, 1))
    pv = np.concatenate([_columns(a["g_mix"][0]), _columns(a["g_x"][0]), _columns(a["g_ffn"][0]), conv,
                         _columns(a["s_pool"][0]), bs, bs8], axis=1)
    pad = np.full(8 - NG, NEG, f)
    row = np.concatenate([a["ln_a_g"][0], a["ln_a_b"][0], a["b_rg"][0], pad, a["b_re"][0].reshape(-1)])
    wr = np.concatenate([a["w_rg"][0], np.zeros((D, 8 - NG), f), a["w_re"][0].reshape(D, NE)], axis=1)
    e1 = a["w_e1"][0].reshape(NE, KD, P, FE)
    e3 = a["w_e3"][0].reshape(NE, KD, P, FE)
    e2 = a["w_e2"][0].reshape(NE, 2, P, D)
    we = np.empty((NE, P, 6144), f)
    we[:, :, :4096] = np.concatenate([e1, e3], axis=3).transpose(0, 2, 1, 3).reshape(NE, P, 4096)
    we[:, :, 4096:] = e2.transpose(0, 2, 1, 3).reshape(NE, P, 2048)
    return {
        "x_prompt": a["x_prompt"], "x_sample": a["x_sample"], 
        "state_conv": a["state_conv"], "state_pool": a["state_pool"],
        "cache_mem_v": a["cache_mem_v"],
        "cst": _constants(), "pv": pv, "rv": np.broadcast_to(row, (P, row.size)),
        "gfin": np.broadcast_to(a["g_final"], (P, D)),
        "wpool": wp, "w8": w8.reshape(TS, AH, TS), "ws": a["w_s"][0].transpose(1, 0, 2),
        "wr": _tiles(wr), "wu": _tiles(w_in[:, :DA]), "wv": _tiles(w_in[:, DA:2 * DA]),
        "xt": _features(np.concatenate([a["x_prompt"][0], a["x_sample"].reshape(TS, D)])),
        "memt": _features(a["mem_prompt"][0]),
        "kct": np.stack([_features(a["cache_mem_k"][0, b].reshape(MEM, D)) for b in range(NB)]),
        "wbc": np.stack([_tiles(w_in[:, c:c + P]) for c in starts]),
        "wo": _tiles(a["w_out"][0]), "wk": _tiles(a["w_xk"][0]), "wvx": _tiles(a["w_xv"][0]),
        "wq": np.stack([_tiles(a["w_xq"][0][:, P * k:P * k + P]) for k in range(KD)]), "wxo": _tiles(a["w_xo"][0]), "we": we,
    }


def kernel(**inputs):
    import concourse.bacc as bacc
    from concourse.bass_utils import run_bass_kernel_spmd

    nc = bacc.Bacc("TRN2", target_bir_lowering=False, num_devices=1)
    arrays = {k: np.ascontiguousarray(v) for k, v in
              _layouts({k: np.asarray(v) for k, v in inputs.items()}).items()}
    ins = {k: nc.dram_tensor(f"in_{k}", v.shape, F32, kind="ExternalInput").ap() for k, v in arrays.items()}
    outs = {k: nc.dram_tensor(f"out_{k}", s, F32, kind="ExternalOutput").ap() for k, s in _OUTS}
    trunk_step(nc, ins, outs)
    r = run_bass_kernel_spmd(nc, [{f"in_{k}": v for k, v in arrays.items()}], core_ids=[0])
    return tuple(r.results[0][f"out_{k}"] for k, _ in _OUTS)
```
